# Optimizing a Trainium2 kernel written in Bass

```python
import math
import jax, jax.numpy as jnp
from jax import lax
import numpy as np

D_MODEL = 2048
BATCH = 1
SEQ = 256
DEPTH = 1
DEC_BATCH = 1
DEC_SEQ = 1024
PAST_LEN = 512

GRID_W = 64
NA_HEADS = 16
HEAD_DIM = 64
NA_WIDTH = NA_HEADS * HEAD_DIM
POOL_WINDOWS = (2, 4, 8, 16)
N_POOL = len(POOL_WINDOWS)
POOL_WIDTH = D_MODEL // 2
POOL_GROUP = POOL_WIDTH // N_POOL
MIX_WIDTH = NA_WIDTH + POOL_WIDTH
IN_WIDTH = 3 * NA_WIDTH + POOL_WIDTH
NA_MAX_ROWS = 8
NA_COLS = 16
Q_BLOCK_ROWS_MAX = 8
Q_BLOCK_COLS = 16
CTX_Q_BLOCK = 128
N_EXPERTS = 16
EC_CAPACITY_FACTOR = 2
D_EXPERT = 1024
N_MOD = 6
RMS_EPS = 1e-6
NEG_INF = -1e30

kernel_name = "hybrid_na_pool_ec_diffusion_step"

def rms_norm(x, gain):
    xf = x.astype(jnp.float32)
    y = xf * lax.rsqrt(jnp.mean(xf * xf, axis=-1, keepdims=True) + RMS_EPS)
    return (y * gain.astype(jnp.float32)).astype(x.dtype)

def adaln(cond, w_mod, b_mod):
    m = jax.nn.silu(cond) @ w_mod + b_mod
    return jnp.split(m, N_MOD, axis=-1)

def modulate(h, shift, scale):
    return h * (1 + scale[:, None]) + shift[:, None]

def mixer_proj(h, w_in):
    B, T = h.shape[:2]
    p = h @ w_in
    q, k, v, u = jnp.split(p, [NA_WIDTH, 2 * NA_WIDTH, 3 * NA_WIDTH], axis=-1)
    hd = lambda a: a.reshape(B, T, NA_HEADS, HEAD_DIM)
    return hd(q), hd(k), hd(v), u

def centred_mean(u, w):
    T = u.shape[1]
    uf = u.astype(jnp.float32)
    cs = jnp.concatenate([jnp.zeros_like(uf[:, :1]), jnp.cumsum(uf, axis=1)], axis=1)
    t = jnp.arange(T)
    lo = jnp.maximum(t - w // 2, 0)
    hi = jnp.minimum(t + (w - w // 2), T)
    s = jnp.take(cs, hi, axis=1) - jnp.take(cs, lo, axis=1)
    cnt = (hi - lo).astype(jnp.float32)
    return (s / cnt[None, :, None]).astype(u.dtype)

def pool_mixer(u, w_pool, pool_scale):
    groups = jnp.split(u, N_POOL, axis=-1)
    outs = [(centred_mean(g, w) - g) @ w_pool[i] for i, (g, w) in enumerate(zip(groups, POOL_WINDOWS))]
    return jnp.concatenate(outs, axis=-1) * pool_scale

def context_attention(q, k, v):
    B, S, H, dh = q.shape
    nb = S // CTX_Q_BLOCK
    qb = q.reshape(B, nb, CTX_Q_BLOCK, H, dh).transpose(1, 0, 2, 3, 4)
    scale = HEAD_DIM ** -0.5

    def block(qblk):
        s = jnp.einsum('bqhd,bkhd->bhqk', qblk, k, preferred_element_type=jnp.float32) * scale
        p = jax.nn.softmax(s, axis=-1).astype(v.dtype)
        return jnp.einsum('bhqk,bkhd->bqhd', p, v)

    o = lax.map(block, qb)
    return o.transpose(1, 0, 2, 3, 4).reshape(B, S, H * dh)

def neighbourhood_attention(q, k, v, k_ctx, v_ctx, rpb):
    B, T, H, dh = q.shape
    rows = T // GRID_W
    kh = min(NA_MAX_ROWS, rows)
    kw = NA_COLS
    qbh = math.gcd(rows, Q_BLOCK_ROWS_MAX)
    qbw = Q_BLOCK_COLS
    kr = min(rows, kh + qbh - 1)
    kbw = min(GRID_W, kw + qbw - 1)
    nrb = rows // qbh
    ncb = GRID_W // qbw
    row_start = jnp.clip(jnp.arange(rows) - kh // 2, 0, rows - kh)
    col_start = jnp.clip(jnp.arange(GRID_W) - kw // 2, 0, GRID_W - kw)
    blk_row0 = jnp.clip(jnp.arange(nrb) * qbh - kh // 2, 0, rows - kr)
    blk_col0 = jnp.clip(jnp.arange(ncb) * qbw - kw // 2, 0, GRID_W - kbw)
    key_rows = blk_row0[:, None] + jnp.arange(kr)
    key_cols = blk_col0[:, None] + jnp.arange(kbw)
    q_rows = jnp.arange(nrb)[:, None] * qbh + jnp.arange(qbh)
    q_cols = jnp.arange(ncb)[:, None] * qbw + jnp.arange(qbw)
    rs = row_start[q_rows][:, :, None]
    cs = col_start[q_cols][:, :, None]
    in_row = (key_rows[:, None, :] >= rs) & (key_rows[:, None, :] < rs + kh)
    in_col = (key_cols[:, None, :] >= cs) & (key_cols[:, None, :] < cs + kw)
    d_row = jnp.clip(key_rows[:, None, :] - q_rows[:, :, None] + (NA_MAX_ROWS - 1), 0, 2 * NA_MAX_ROWS - 2)
    d_col = jnp.clip(key_cols[:, None, :] - q_cols[:, :, None] + (NA_COLS - 1), 0, 2 * NA_COLS - 2)
    mask = in_row[:, None, :, None, :, None] & in_col[None, :, None, :, None, :]
    bias = rpb[:, d_row[:, None, :, None, :, None], d_col[None, :, None, :, None, :]].astype(jnp.float32)
    bias = jnp.where(mask[None], bias, NEG_INF).reshape(H, nrb, ncb, qbh * qbw, kr * kbw)

    qb = q.reshape(B, nrb, qbh, ncb, qbw, H, dh).transpose(0, 1, 3, 2, 4, 5, 6).reshape(B, nrb, ncb, qbh * qbw, H, dh)
    ri = key_rows[:, None, :, None]
    ci = key_cols[None, :, None, :]
    kg = k.reshape(B, rows, GRID_W, H, dh)[:, ri, ci].reshape(B, nrb, ncb, kr * kbw, H, dh)
    vg = v.reshape(B, rows, GRID_W, H, dh)[:, ri, ci].reshape(B, nrb, ncb, kr * kbw, H, dh)
    scale = HEAD_DIM ** -0.5
    s_lat = jnp.einsum('bijqhd,bijkhd->bhijqk', qb, kg, preferred_element_type=jnp.float32) * scale + bias[None]
    s_ctx = jnp.einsum('bijqhd,bkhd->bhijqk', qb, k_ctx, preferred_element_type=jnp.float32) * scale
    n_lat = kr * kbw
    p = jax.nn.softmax(jnp.concatenate([s_lat, s_ctx], axis=-1), axis=-1).astype(v.dtype)
    o = (jnp.einsum('bhijqk,bijkhd->bijqhd', p[..., :n_lat], vg)
         + jnp.einsum('bhijqk,bkhd->bijqhd', p[..., n_lat:], v_ctx))
    o = o.reshape(B, nrb, ncb, qbh, qbw, H, dh).transpose(0, 1, 3, 2, 4, 5, 6)
    return o.reshape(B, T, H * dh)

def expert_choice_ffn(x, w_router, w_gate, w_up, w_down):
    B, n, D = x.shape
    cap = EC_CAPACITY_FACTOR * n // N_EXPERTS
    logits = jnp.einsum('bnd,de->ben', x, w_router, preferred_element_type=jnp.float32)
    aff = jax.nn.softmax(logits, axis=1)
    g, idx = lax.top_k(aff, cap)
    xs = jax.vmap(lambda xb, ib: xb[ib])(x, idx)
    hcur = jax.nn.silu(jnp.einsum('becd,edf->becf', xs, w_gate)) * jnp.einsum('becd,edf->becf', xs, w_up)
    ys = jnp.einsum('becf,efd->becd', hcur, w_down) * g[..., None].astype(x.dtype)
    return jax.vmap(lambda yb, ib: jnp.zeros((n, D), yb.dtype).at[ib.reshape(-1)].add(yb.reshape(-1, D)))(ys, idx)

def setup_inputs(seed: int = 0) -> dict:
    key = jax.random.key(seed)
    ks = jax.random.split(key, 20)
    nrm = lambda k, shape, s: jax.random.normal(k, shape, jnp.float32) * s
    return {
        'x_prompt': nrm(ks[0], (BATCH, SEQ, D_MODEL), 1.0),
        'x_sample': nrm(ks[1], (DEC_BATCH, DEC_SEQ, D_MODEL), 1.0),
        'cache_k': nrm(ks[2], (DEC_BATCH, DEPTH, PAST_LEN, NA_HEADS, HEAD_DIM), 1.0),
        'cache_v': nrm(ks[3], (DEC_BATCH, DEPTH, PAST_LEN, NA_HEADS, HEAD_DIM), 1.0),
        'c': nrm(ks[4], (DEC_BATCH, D_MODEL), 1.0),
        'c_ctx': nrm(ks[5], (D_MODEL,), 1.0),
        'w_mod': nrm(ks[6], (DEPTH, D_MODEL, N_MOD * D_MODEL), D_MODEL ** -0.5),
        'b_mod': nrm(ks[7], (DEPTH, N_MOD * D_MODEL), 0.02),
        'norm_mix': 1.0 + nrm(ks[8], (DEPTH, D_MODEL), 0.02),
        'norm_ffn': 1.0 + nrm(ks[9], (DEPTH, D_MODEL), 0.02),
        'w_in': nrm(ks[10], (DEPTH, D_MODEL, IN_WIDTH), D_MODEL ** -0.5),
        'rpb': nrm(ks[11], (DEPTH, NA_HEADS, 2 * NA_MAX_ROWS - 1, 2 * NA_COLS - 1), 0.1),
        'w_pool': nrm(ks[12], (DEPTH, N_POOL, POOL_GROUP, POOL_GROUP), POOL_GROUP ** -0.5),
        'pool_scale': 1.0 + nrm(ks[13], (DEPTH, POOL_WIDTH), 0.1),
        'w_out': nrm(ks[14], (DEPTH, MIX_WIDTH, D_MODEL), MIX_WIDTH ** -0.5),
        'w_router': nrm(ks[15], (DEPTH, D_MODEL, N_EXPERTS), D_MODEL ** -0.5),
        'w_gate': nrm(ks[16], (DEPTH, N_EXPERTS, D_MODEL, D_EXPERT), D_MODEL ** -0.5),
        'w_up': nrm(ks[17], (DEPTH, N_EXPERTS, D_MODEL, D_EXPERT), D_MODEL ** -0.5),
        'w_down': nrm(ks[18], (DEPTH, N_EXPERTS, D_EXPERT, D_MODEL), D_EXPERT ** -0.5),
        'norm_final': 1.0 + nrm(ks[19], (D_MODEL,), 0.02),
    }

def reference(x_prompt, x_sample, cache_k, cache_v, c, c_ctx, w_mod, b_mod, norm_mix, norm_ffn, w_in, rpb,
              w_pool, pool_scale, w_out, w_router, w_gate, w_up, w_down, norm_final):
    yp = x_prompt
    ys = x_sample
    new_k_layers = []
    new_v_layers = []
    for l in range(DEPTH):
        m_ctx = adaln(c_ctx[None], w_mod[l], b_mod[l])
        m_lat = adaln(c, w_mod[l], b_mod[l])

        h = modulate(rms_norm(yp, norm_mix[l]), m_ctx[0], m_ctx[1])
        q, k, v, u = mixer_proj(h, w_in[l])
        new_k_layers.append(k)
        new_v_layers.append(v)
        mix = jnp.concatenate([context_attention(q, k, v), pool_mixer(u, w_pool[l], pool_scale[l])], axis=-1) @ w_out[l]
        yp = yp + m_ctx[2][:, None] * mix
        h = modulate(rms_norm(yp, norm_ffn[l]), m_ctx[3], m_ctx[4])
        yp = yp + m_ctx[5][:, None] * expert_choice_ffn(h, w_router[l], w_gate[l], w_up[l], w_down[l])

        h = modulate(rms_norm(ys, norm_mix[l]), m_lat[0], m_lat[1])
        q, k, v, u = mixer_proj(h, w_in[l])
        att = neighbourhood_attention(q, k, v, cache_k[:, l], cache_v[:, l], rpb[l])
        mix = jnp.concatenate([att, pool_mixer(u, w_pool[l], pool_scale[l])], axis=-1) @ w_out[l]
        ys = ys + m_lat[2][:, None] * mix
        h = modulate(rms_norm(ys, norm_ffn[l]), m_lat[3], m_lat[4])
        ys = ys + m_lat[5][:, None] * expert_choice_ffn(h, w_router[l], w_gate[l], w_up[l], w_down[l])

    y_prompt = rms_norm(yp, norm_final)
    y_sample = rms_norm(ys, norm_final)
    new_k = jnp.stack(new_k_layers, axis=1)
    new_v = jnp.stack(new_v_layers, axis=1)
    return (y_prompt, y_sample, new_k, new_v)


_drawn_inputs = setup_inputs


def setup_inputs(seed=0):
    import zlib

    import numpy as np

    out = dict(_drawn_inputs(seed))
    spreads = {}
    factors = {'norm_mix': 2.837,
     'rpb': 8.0,
     'norm_final': 8.427,
     'cache_k': 8.0,
     'cache_v': 8.0,
     'norm_ffn': 4.887}
    for name, (base, spread) in spreads.items():
        noise = np.random.default_rng([zlib.crc32(name.encode()), seed]).standard_normal(out[name].shape)
        drawn = base * np.exp(spread * noise) if base else spread * noise
        out[name] = __import__('jax').numpy.asarray(drawn.astype(out[name].dtype))
    for name, factor in factors.items():
        out[name] = (out[name] * factor).astype(out[name].dtype)
    return out
```

```python
from contextlib import ExitStack

import numpy as np

import concourse.bass as bass
from concourse import mybir

ACT = mybir.ActivationFunctionType
ALU = mybir.AluOpType
AX = mybir.AxisListType
F32 = mybir.dt.float32
F32R = mybir.dt.float32r
U32 = mybir.dt.uint32
ds = bass.ds

P = 128
D = 2048
KD = D // P
LAT, CTX = 1024, 256
TOK = LAT + CTX
PAST = 512
H, DH = 16, 64
NA_W = H * DH
IN_W = 4096
MIX_W = 2048
GRID_W, ROWS = 64, 16
WIN_R, WIN_C = 8, 16
QR, QC = 8, 16
KR, KC = 12, 32
NKL = KR * KC
NKEY = NKL + PAST
E = 16
FE = 1024
KF = FE // P
CAP_L, CAP_C = 2 * LAT // E, 2 * CTX // E
CAP = CAP_L + CAP_C
EPS = 1e-6
POOLW = (2, 4, 8, 16)
GT = TOK // 2
HT = GT // 2
TPG = GT // P
CH = 4096
CW = CH // KD
AHEAD = 1
FIRST = 16
COLB = (0, 8, 24, 32)
KIND = (0, 1, 1, 2)
BOFF = (16, 8, 0)


def block_diffusion_step(nc, xcat, condT, bmodT, normmT, normfT, nfin, poolsT, w_mod, w_in, wpool,
                         w_out, wrT, w_gate, w_up, w_down, kcT, vcache, biasE, masks, invcnt, identity,
                         y_prompt, y_sample, new_k, new_v):
    projT = nc.dram_tensor("projT", [IN_W, TOK], F32, kind="Internal").ap()
    mixhi_d = nc.dram_tensor("mixhi", [MIX_W, TOK], F32, kind="Internal").ap()
    mixlo_d = nc.dram_tensor("mixlo", [MIX_W, TOK], F32, kind="Internal").ap()
    mean_d = nc.dram_tensor("window_mean_less_u", [D - NA_W, TOK], F32, kind="Internal").ap()
    y_d = nc.dram_tensor("y_resid", [TOK, D], F32, kind="Internal").ap()
    xn_d = nc.dram_tensor("x_ffn_normed", [TOK, D], F32, kind="Internal").ap()

    with ExitStack() as top:
        def sem(name):
            return top.enter_context(nc.semaphore(name))

        def sb(name, shape, dt=F32):
            return top.enter_context(nc.sbuf_tensor(name, shape, dt))

        ps = top.enter_context(nc.psum_tensor("ps", [P, 8, 512], F32))
        ident = sb("ident", [P, P])
        modT = sb("modT", [P, 96, 2])
        bmod = sb("bmod", [P, 96, 2])
        cT = sb("cT", [P, KD, 2])
        ones = sb("ones", [P, 1])
        nmT = sb("nmT", [P, KD])
        nfT = sb("nfT", [P, KD])
        mulT = sb("mulT", [P, 2, KD])
        addT = sb("addT", [P, 2, KD])

        mod_first(nc, sem, locals())
        input_projection(nc, sem, locals())
        attention(nc, sem, locals())
        output_projection(nc, sem, locals())
        with ExitStack() as route:
            top_route = route
            idxL = route.enter_context(nc.sbuf_tensor("idxL", [P, E + 1], U32))
            idxC = route.enter_context(nc.sbuf_tensor("idxC", [P, E + 1], U32))
            gL = route.enter_context(nc.sbuf_tensor("gL", [P, E], F32))
            gC = route.enter_context(nc.sbuf_tensor("gC", [P, E], F32))
            router(nc, sem, locals())
            experts(nc, sem, locals())
        final_norm(nc, sem, locals())


def w_chunk(w, col, width=CW):
    return w[:, ds(col, width)].rearrange("(k p) n -> p k n", p=P)


def mod_first(nc, sem, v):
    ps, ident, modT, bmod, cT, nmT, mulT, addT = (v[n] for n in
                                                  ("ps", "ident", "modT", "bmod", "cT", "nmT", "mulT", "addT"))
    NCH = 2 * D // CW
    consts_in = sem("m_consts_in")
    chunk_in = [sem(f"m_chunk_in{s}") for s in range(2)]
    cond_ready = sem("m_cond_ready")
    chunk_used = sem("m_chunk_used")
    row_made = sem("m_row_made")
    row_turned = sem("m_row_turned")
    mod_read = sem("m_mod_read")
    with nc.sbuf_tensor("m_raw", [P, 2, CH], F32) as raw, nc.sbuf_tensor("m_row", [2, 2, CW], F32) as row, \
            nc.Block() as block:
        @block.sync
        def _(sp):
            for dst, src in ((ident, v["identity"]), (cT, v["condT"]), (bmod, v["bmodT"]), (nmT, v["normmT"]),
                             (v["nfT"], v["normfT"])):
                sp.dma_start(dst[:], src).then_inc(consts_in, 16)
            for s in range(2):
                sp.dma_start(raw[:, s, :].rearrange("p (k n) -> p k n", k=KD),
                             w_chunk(v["w_mod"], s * CW)).then_inc(chunk_in[s], 16)
            with sp.Fori(1, NCH // 2) as i:
                for s in range(2):
                    sp.wait_ge(chunk_used, i * 2 + s - 1)
                    sp.dma_start(raw[:, s, :].rearrange("p (k n) -> p k n", k=KD),
                                 w_chunk(v["w_mod"], i * 2 * CW + s * CW)).then_inc(chunk_in[s], 16)

        @block.scalar
        def _(act):
            act.wait_ge(consts_in, 80)
            nc.scalar.activation(cT[:], cT[:], ACT.Silu).then_inc(cond_ready, 1)

        @block.tensor
        def _(pe):
            pe.wait_ge(cond_ready, 1)
            with pe.Fori(0, NCH // 2) as i:
                for s in range(2):
                    pe.wait_ge(chunk_in[s], i * 16 + 16)
                    pe.wait_ge(mod_read, i * 2 + s + 1)
                    for k in range(KD):
                        last = nc.tensor.matmul(ps[0:2, s, 0:CW], cT[:, k, :], raw[:, s, k * CW:k * CW + CW],
                                                start=(k == 0), stop=(k == KD - 1))
                    last.then_inc(chunk_used, 1)
                    pe.wait_ge(row_made, i * 2 + s + 1)
                    for b in range(CW // P):
                        last = nc.tensor.matmul(ps[:, 2 + s, 2 * b:2 * b + 2], row[:, s, b * P:b * P + P],
                                                ident[0:2, 0:2], start=True, stop=True)
                    last.then_inc(row_turned, 1)

        @block.vector
        def _(dve):
            dve.wait_ge(consts_in, 80)
            nc.vector.memset(v["ones"][:], 1.0)
            nc.vector.memset(mulT[:], 0.0).then_inc(mod_read, 2)
            with dve.Fori(0, NCH // 2) as i:
                for s in range(2):
                    dve.wait_ge(chunk_used, i * 2 + s + 1)
                    nc.vector.tensor_copy(row[:, s, :], ps[0:2, s, 0:CW]).then_inc(row_made, 1)
                    dve.wait_ge(row_turned, i * 2 + s + 1)
                    nc.vector.tensor_tensor(modT[:, ds(i * 4 + s * 2, 2), :],
                                            ps[:, 2 + s, 0:4].rearrange("p (b c) -> p b c", c=2),
                                            bmod[:, ds(i * 4 + s * 2, 2), :], ALU.add).then_inc(mod_read, 1)
            dve.wait_ge(mod_read, NCH + 2)
            for c in range(2):
                nc.vector.tensor_copy(addT[:, c, :], modT[:, 0:KD, c])
                nc.vector.scalar_tensor_tensor(out=mulT[:, c, :], in0=modT[:, KD:2 * KD, c], scalar=1.0,
                                               in1=nmT[:], op0=ALU.add, op1=ALU.mult)


def input_projection(nc, sem, v):
    ps, ident, modT, bmod, cT, mulT, addT = (v[n] for n in ("ps", "ident", "modT", "bmod", "cT", "mulT", "addT"))
    xcat, projT, w_in, w_mod, ones = v["xcat"], v["projT"], v["w_in"], v["w_mod"], v["ones"]
    NCH = IN_W // CW
    NP = 4
    SLOTS = 2 * NP
    MB0 = 2 * KD
    x_in = [sem(f"p_x_in{s}") for s in range(2)]
    x_square = sem("p_x_square")
    x_rms = sem("p_x_rms")
    x_scaled = sem("p_x_scaled")
    x_turned = sem("p_x_turned")
    h_step = sem("p_h_step")
    h_hi = sem("p_h_hi")
    h_made = sem("p_h_made")
    w_loaded = [sem(f"p_w_loaded{s}") for s in range(2)]
    w_hi_made = sem("p_w_hi_made")
    w_lo_made = sem("p_w_lo_made")
    piece_used = sem("p_piece_used")
    sums_read = sem("p_sums_read")
    stored = [sem(f"p_stored{s}") for s in range(2)]
    mod_in = sem("p_mod_in")
    mod_step = sem("p_mod_step")
    mod_turned = sem("p_mod_turned")
    mod_read = sem("p_mod_read")
    with ExitStack() as ctx:
        def sb(name, shape, dt=F32):
            return ctx.enter_context(nc.sbuf_tensor(name, shape, dt))
        hhi = sb("hhi", [P, KD, GT], F32R)
        hlo = sb("hlo", [P, KD, GT], F32R)
        raw = sb("p_raw", [P, 2, CH])
        whi = sb("p_whi", [P, 2, CH], F32R)
        wlo = sb("p_wlo", [P, 2, CH], F32R)
        modraw = sb("p_modraw", [P, CH])
        xt = modraw[:].rearrange("p (s d) -> p s d", s=2)
        out_st = sb("p_out_st", [P, 2, GT])
        tmp = sb("p_tmp", [P, 2, 512])
        acc = sb("p_acc", [P, 2, CW])
        stat = sb("p_stat", [P, 2, 2])
        block = ctx.enter_context(nc.Block())

        def piece(t, s, q):
            b, half = divmod(q, 2)
            return t[:, s, :].rearrange("p (k n) -> p k n", k=KD)[:, half * 8:half * 8 + 8, b * P:b * P + P]

        def slot(t, s):
            return t[:, s, :].rearrange("p (k n) -> p k n", k=KD)

        @block.sync
        def _(sp):
            def load_w(g, n, s):
                sp.wait_ge(w_lo_made, g * (NCH * NP) + n * NP + NP)
                sp.dma_start(slot(raw, s), w_chunk(w_in, n * CW)).then_inc(w_loaded[s], 16)

            def load_mod(g, n):
                sp.wait_ge(mod_step, g * (2 * KD * NCH) + n * (2 * KD) + AHEAD)
                sp.dma_start(modraw[:].rearrange("p (k n) -> p k n", k=KD),
                             w_chunk(w_mod, g * (NCH * CW) + n * CW + MB0 * P)).then_inc(mod_in, 16)

            for s in (mod_step, mod_turned):
                sp.sem_inc(s, AHEAD)
            with sp.Fori(0, 2) as g:
                sp.wait_ge(mod_step, g * (2 * KD * NCH) + AHEAD)
                for t in range(TPG):
                    if t >= 2:
                        sp.wait_ge(x_turned, g * (4 * TPG) + 4 * (t - 1))
                    sp.dma_start(xt[:, t % 2, :], xcat[ds(g * GT + t * P, P), :]).then_inc(x_in[t % 2], 16)
                    if t < 2:
                        load_w(g, t, t)
                sp.wait_ge(x_turned, g * (4 * TPG) + 4 * TPG)
                load_mod(g, 0)
                with sp.Fori(1, NCH // 2) as i:
                    for s in range(2):
                        load_w(g, i * 2 + s, s)
                        load_mod(g, i * 2 + (s - 1))
                load_mod(g, NCH - 1)

        @block.gpsimd
        def _(pool):
            for b in range(2):
                pool.dma_start(out_st[:, b, 0:KD], v["normmT"]).then_inc(stored[b], 16)
            with pool.Fori(0, 2) as g:
                with pool.Fori(0, NCH) as n:
                    for b in range(2):
                        pool.wait_ge(sums_read, g * (NCH * 4) + n * 4 + (2 * b + 2 + 4))
                        pool.dma_start(projT[ds(n * CW + b * P, P), ds(g * GT, GT)], out_st[:, b, :]
                                       ).then_inc(stored[b], 16)
            for b in range(2):
                pool.wait_ge(stored[b], 2 * NCH * 16 + FIRST)

        @block.scalar
        def _(act):
            def square(g, t):
                act.wait_ge(x_in[t % 2], g * (16 * (3 - t % 2)) + 16 * (t // 2 + 1))
                if t == 0:
                    act.wait_ge(mod_read, g * NCH + 1)
                nc.scalar.activation(ps[:, 4:8, :].rearrange("p b n -> p (b n)"), xt[:, t % 2, :], ACT.Square,
                                     accum_out=stat[:, t % 2, 0:1]).then_inc(x_square, 1)
                act.wait_ge(x_rms, g * (3 * TPG) + 3 * t + 1)
                nc.scalar.activation(stat[:, t % 2, 1:2], stat[:, t % 2, 0:1], ACT.Sqrt).then_inc(x_rms, 1)

            def make_hi(g, n, s):
                act.wait_ge(w_loaded[s], g * (8 * NCH) + (n - s) * 8 + 16)
                for q in range(NP):
                    act.wait_ge(piece_used, g * (NCH * NP) + n * NP + (q + 1))
                    nc.scalar.activation(piece(whi, s, q), piece(raw, s, q), ACT.Copy).then_inc(w_hi_made, 1)

            with act.Fori(0, 2) as g:
                square(g, 0)
                for t in range(TPG):
                    if t + 1 < TPG:
                        square(g, t + 1)
                    for b in range(4):
                        act.wait_ge(h_step, g * (8 * TPG) + 8 * t + 2 * (b + 1))
                        nc.scalar.activation(hhi[:, 4 * b:4 * b + 4, t * P:t * P + P],
                                             tmp[:, b % 2, :].rearrange("p (k n) -> p k n", k=4), ACT.Copy
                                             ).then_inc(h_hi, 1)
                with act.Fori(0, NCH // 2) as i:
                    for s in range(2):
                        make_hi(g, i * 2 + s, s)

        @block.vector
        def _(dve):
            for n, (what, credit) in enumerate(((piece_used, SLOTS), (w_lo_made, SLOTS), (sums_read, 4),
                                                (mod_read, 1))):
                nc.vector.memset(tmp[:, 0, 64 * n:64 * n + 64], 0.0).then_inc(what, credit)
            dve.wait_ge(mod_read, 1)

            def scale_tile(g, t):
                st = stat[:, t % 2, :]
                at = g * (3 * TPG) + 3 * t
                dve.wait_ge(x_square, g * TPG + t + 1)
                nc.vector.tensor_scalar(st[:, 0:1], st[:, 0:1], 1.0 / D, EPS, ALU.mult, ALU.add).then_inc(x_rms, 1)
                dve.wait_ge(x_rms, at + 2)
                nc.vector.reciprocal(st[:, 0:1], st[:, 1:2]).then_inc(x_rms, 1)
                dve.wait_ge(x_rms, at + 3)
                nc.vector.tensor_scalar(xt[:, t % 2, :], xt[:, t % 2, :], st[:, 0:1], None, ALU.mult
                                        ).then_inc(x_scaled, 1)

            def modulate_tile(g, t):
                c = g if t >= 3 else 0

                def multiply_add(b):
                    dve.wait_ge(x_turned, g * (4 * TPG) + 4 * t + b + 1)
                    if t or b >= 2:
                        dve.wait_ge(h_made, g * (4 * TPG) + 4 * t + b - 1)
                    m, a = (x[:, ds(c, 1), 4 * b:4 * b + 4].rearrange("p a k -> p (a k)").unsqueeze(2)
                            .broadcast_to([P, 4, P]) for x in (mulT, addT))
                    t3 = tmp[:, b % 2, :].rearrange("p (k n) -> p k n", k=4)
                    nc.vector.tensor_tensor(t3, ps[:, b, :].rearrange("p (k n) -> p k n", k=4), m, ALU.mult
                                            ).then_inc(h_step, 1)
                    dve.wait_ge(h_step, g * (8 * TPG) + 8 * t + 2 * b + 1)
                    nc.vector.tensor_tensor(t3, t3, a, ALU.add).then_inc(h_step, 1)

                multiply_add(0)
                for b in range(4):
                    if b < 3:
                        multiply_add(b + 1)
                    dve.wait_ge(h_hi, g * (4 * TPG) + 4 * t + b + 1)
                    nc.vector.tensor_tensor(hlo[:, 4 * b:4 * b + 4, t * P:t * P + P],
                                            tmp[:, b % 2, :].rearrange("p (k n) -> p k n", k=4),
                                            hhi[:, 4 * b:4 * b + 4, t * P:t * P + P].bitcast(F32),
                                            ALU.subtract).then_inc(h_made, 1)

            def make_lo(g, n, s):
                for q in range(NP):
                    dve.wait_ge(w_hi_made, g * (NCH * NP) + n * NP + (q + 1))
                    nc.vector.tensor_tensor(piece(wlo, s, q), piece(raw, s, q), piece(whi, s, q).bitcast(F32),
                                            ALU.subtract).then_inc(w_lo_made, 1)

            def copy_sum(g, n, b):
                dve.wait_ge(piece_used, g * (NCH * NP) + n * NP + (2 * b + 2 + SLOTS))
                dve.wait_ge(stored[b], g * (NCH * 16) + n * 16 + FIRST)
                for half in range(2):
                    nc.vector.tensor_copy(out_st[:, b, half * HT:half * HT + HT],
                                          ps[:, 2 * b + half, 0:HT]).then_inc(sums_read, 1)

            def mod_sums(g, n):
                dve.wait_ge(mod_in, g * (NCH * 16) + n * 16 + 16)
                dve.wait_ge(mod_turned, g * NCH + n + AHEAD)
                for k in range(KD):
                    for c in range(2):
                        w = modraw[:, k * CW:(k + 1) * CW]
                        if k == 0:
                            ins = nc.vector.tensor_scalar(acc[:, c, :], w, cT[:, k, c:c + 1], None, ALU.mult)
                        else:
                            dve.wait_ge(mod_step, g * (2 * KD * NCH) + n * (2 * KD) + 2 * (k - 1) + c + 1 + AHEAD)
                            ins = nc.vector.scalar_tensor_tensor(out=acc[:, c, :], in0=w,
                                                                 scalar=cT[:, k, c:c + 1], in1=acc[:, c, :],
                                                                 op0=ALU.mult, op1=ALU.add)
                        ins.then_inc(mod_step, 1)

            def chunk(g, n, s, following=True):
                mod_sums(g, n)
                copy_sum(g, n, 0)
                if following:
                    make_lo(g, n + 1, 1 - s)
                copy_sum(g, n, 1)
                dve.wait_ge(mod_turned, g * NCH + n + 1 + AHEAD)
                at = g * (2 * NCH) + n * 2 + MB0
                nc.vector.tensor_tensor(modT[:, ds(at, 2), :], ps[:, 4, 0:4].rearrange("p (b c) -> p b c", c=2),
                                        bmod[:, ds(at, 2), :], ALU.add).then_inc(mod_read, 1)

            with dve.Fori(0, 2) as g:
                scale_tile(g, 0)
                for t in range(TPG):
                    if t + 1 < TPG:
                        scale_tile(g, t + 1)
                    modulate_tile(g, t)
                make_lo(g, 0, 0)
                with dve.Fori(0, NCH // 2 - 1) as i:
                    for s in range(2):
                        chunk(g, i * 2 + s, s)
                chunk(g, NCH - 2, 0)
                chunk(g, NCH - 1, 1, False)

        @block.tensor
        def _(pe):
            with pe.Fori(0, 2) as g:
                for t in range(TPG):
                    pe.wait_ge(x_scaled, g * TPG + t + 1)
                    for b in range(4):
                        if t == 0 and b == 0:
                            pe.wait_ge(sums_read, g * (NCH * 4) + 4)
                        elif t:
                            pe.wait_ge(h_step, g * (8 * TPG) + 8 * (t - 1) + 2 * b + 1)
                        for k in range(4):
                            kk = 4 * b + k
                            last = nc.tensor.transpose(ps[:, b, k * P:k * P + P],
                                                       xt[:, t % 2, kk * P:kk * P + P], ident[:])
                        last.then_inc(x_turned, 1)
                with pe.Fori(0, NCH // 2) as i:
                    pe.wait_ge(h_made, g * (4 * TPG) + 4 * TPG)
                    for s in range(2):
                        for b in range(2):
                            pe.wait_ge(sums_read, g * (NCH * 4) + i * 8 + (s * 4 + 2 * b + 2))
                            for k in range(KD):
                                if k % 8 == 0:
                                    pe.wait_ge(w_lo_made, g * (NCH * NP) + i * (2 * NP)
                                               + (s * NP + 2 * b + k // 8 + 1 + SLOTS))
                                wh = whi[:, s, k * CW + b * P:k * CW + b * P + P]
                                wl = wlo[:, s, k * CW + b * P:k * CW + b * P + P]
                                for j, (w, hx) in enumerate(((wh, hhi), (wh, hlo), (wl, hhi))):
                                    for half in range(2):
                                        last = nc.tensor.matmul(ps[:, 2 * b + half, 0:HT], w,
                                                                hx[:, k, half * HT:half * HT + HT],
                                                                start=(k == 0 and j == 0),
                                                                stop=(k == KD - 1 and j == 2))
                                if k % 8 == 7:
                                    last.then_inc(piece_used, 1)
                        pe.wait_ge(mod_step, g * (2 * KD * NCH) + i * (4 * KD) + (s + 1) * 2 * KD + AHEAD)
                        pe.wait_ge(mod_read, g * NCH + i * 2 + (s + 1))
                        for b in range(2):
                            for c in range(2):
                                last = nc.tensor.matmul(ps[:, 4, 2 * b + c:2 * b + c + 1],
                                                        acc[:, c, b * P:b * P + P], ones[:],
                                                        start=True, stop=True)
                        last.then_inc(mod_turned, 1)


def attention(nc, sem, v):
    ps, ident, projT = v["ps"], v["ident"], v["projT"]
    J = H // 2
    W = 10
    LW = 8
    U = 2 * W
    CB = CTX // P
    KCOL = TOK + PAST
    NB = 5
    mask_in = sem("a_mask_in")
    kq_in = sem("a_kq_in")
    q_scaled = sem("a_q_scaled")
    q_hi_made = sem("a_q_hi_made")
    k_hi_made = sem("a_k_hi_made")
    q_lo_made = sem("a_q_lo_made")
    k_lo_made = sem("a_k_lo_made")
    vc_in = [sem(f"a_vc_in{h}") for h in range(2)]
    v_in = sem("a_v_in")
    v_laid = sem("a_v_laid")
    kx_in = sem("a_kx_in")
    bias_in = [sem(f"a_bias_in{h}") for h in range(2)]
    bias_made = sem("a_bias_made")
    scored = sem("a_scored")
    maxed = sem("a_maxed")
    negmax_ready = sem("a_negmax_ready")
    exped = sem("a_exped")
    summed = sem("a_summed")
    inverted = sem("a_inverted")
    probs_ready = sem("a_probs_ready")
    turned = sem("a_turned")
    copied_a = sem("a_copied_a")
    copied_b = sem("a_copied_b")
    valued = sem("a_valued")
    out_hi = sem("a_out_hi")
    out_lo = sem("a_out_lo")
    batch_turned = sem("a_batch_turned")
    batch_read = sem("a_batch_read")
    att_stored = [sem(f"a_att_stored{h}") for h in range(2)]
    newk_stored = sem("a_newk_stored")
    newv_stored = sem("a_newv_stored")
    u_in = sem("a_u_in")
    pool_step = sem("a_pool_step")
    mean_stored = sem("a_mean_stored")
    PADL = 8
    SEG = ((PADL, 0, LAT), (PADL + LAT + 2 * PADL, LAT, CTX))
    PW = LAT + CTX + 4 * PADL

    def unit(u):
        h, w = divmod(u % U, W)
        return (h, True, w) if w < LW else (h, False, w - LW)

    def lat_before(u):
        return LW * (u // W) + min(u % W, LW)

    def maxed_before(u):
        return u + lat_before(u)

    with ExitStack() as ctx:
        def sb(name, shape, dt=F32):
            return ctx.enter_context(nc.sbuf_tensor(name, shape, dt))
        mask = sb("mask", [P, 6, NKL])
        brow = sb("brow", [P, 2, 16 * 48])
        bias = sb("bias", [P, 2, 6, NKL])
        vc = sb("vc", [P, PAST // P, P])
        qraw = sb("qraw", [P, TOK])
        kraw = sb("kraw", [P, KCOL])
        q8 = sb("q8", [P, TOK])
        qst = sb("qst", [P, 2, TOK], F32R)
        khh = sb("khh", [P, 2, KCOL], F32R)
        kll = sb("kll", [P, 2, KCOL], F32R)
        vT = sb("vT", [P, TOK])
        vL = sb("vL", [P, 4 * 512 + CTX])
        kx = sb("kx", [P, CTX])
        V = sb("V", [P, 4, 4, P])
        Vx = sb("Vx", [P, CB, P])
        Kx = sb("Kx", [P, CB, P])
        T = sb("T", [P, 2, NKL])
        pr = sb("pr", [P, 4, NKEY])
        prT = sb("prT", [P, 2, NKEY])
        athi = sb("athi", [P, TOK], F32R)
        atlo = sb("atlo", [P, TOK], F32R)
        st = sb("a_st", [P, 4, 8])
        inv = sb("inv", [P, TOK])
        pu = sb("pu", [P, PW])
        pc = sb("pc", [P, 2, PW])
        pd = sb("pd", [P, TOK])
        BATCH_AT = {12 + 2 * n: n for n in range(4)}
        block = ctx.enter_context(nc.Block())

        def rows(section, j, first=0, n=TOK):
            return projT[ds(j * P + section * NA_W, P), first:first + n]

        @block.sync
        def _(sp):
            def load_head(j, h):
                sp.wait_ge(q_lo_made, j * 2 + h)
                sp.wait_ge(k_lo_made, j * 2 + h)
                for half in range(2):
                    f = slice(half * DH, half * DH + DH)
                    sp.dma_start(qraw[f, :], projT[ds(j * P + h * DH, DH), :]).then_inc(kq_in, 16)
                    sp.dma_start(kraw[f, 0:TOK], projT[ds(j * P + (NA_W + h * DH), DH), :]).then_inc(kq_in, 16)
                    sp.dma_start(kraw[f, TOK:KCOL], v["kcT"][ds(j * P + h * DH, DH), :]).then_inc(kq_in, 16)

            def load_cached_values(j, h):
                sp.dma_start(vc[:, :, h * DH:h * DH + DH],
                             v["vcache"][:, ds(j * P + h * DH, DH)].rearrange("(b p) f -> p b f", p=P)
                             ).then_inc(vc_in[h], 16)

            def store_outputs(j, h):
                f = slice(h * DH, h * DH + DH)
                for dst, src in ((v["mixhi_d"], athi), (v["mixlo_d"], atlo)):
                    sp.dma_start(dst[ds(j * P + h * DH, DH), :], src[f, :].bitcast(F32)).then_inc(att_stored[h], 16)

            for s in (out_lo, valued, turned, probs_ready, att_stored[0], att_stored[1], newk_stored):
                sp.sem_inc(s, AHEAD)
            load_head(0, 0)
            sp.dma_start(vT[:], rows(2, 0)).then_inc(v_in, 16)
            sp.dma_start(mask[:], v["masks"]).then_inc(mask_in, 16)
            for h in range(2):
                sp.dma_start(brow[:, h, :], v["biasE"][h]).then_inc(bias_in[h], 16)
            for h in range(2):
                load_cached_values(0, h)
            sp.dma_start(kx[:], rows(1, 0, LAT, CTX)).then_inc(kx_in, 16)

            with sp.Fori(0, J) as j:
                load_head(j, 1)
                sp.wait_ge(batch_read, j * NB + NB)
                sp.wait_ge(v_laid, j * 5 + 5)
                sp.dma_start(vT[:], rows(2, j + 1)).then_inc(v_in, 16)
                sp.dma_start(v["new_v"][:, ds(j * P, P)].rearrange("(b p) f -> p b f", p=P), Vx[:]
                             ).then_inc(newv_stored, 16)
                for h in range(2):
                    sp.wait_ge(bias_made, j * 12 + 6 * (h + 1))
                    sp.dma_start(brow[:, h, :], v["biasE"][ds(j * 2 + 2 + h, 1)].rearrange("a p n -> (a p) n")
                                 ).then_inc(bias_in[h], 16)
                load_head(j + 1, 0)
                sp.wait_ge(batch_read, j * NB + (NB + 1))
                sp.wait_ge(out_lo, j * U + W + AHEAD)
                store_outputs(j, 0)
                load_cached_values(j + 1, 0)
                sp.wait_ge(batch_read, j * NB + 2 * NB)
                sp.dma_start(v["new_k"][:, ds(j * P, P)].rearrange("(b p) f -> p b f", p=P), Kx[:]
                             ).then_inc(newk_stored, 16)
                sp.dma_start(kx[:], rows(1, j + 1, LAT, CTX)).then_inc(kx_in, 16)
                load_cached_values(j + 1, 1)
                sp.wait_ge(out_lo, j * U + U + AHEAD)
                store_outputs(j, 1)
            for s, n in ((kq_in, 96 * (2 * J + 1)), (v_in, 16 * (J + 1)), (kx_in, 16 * (J + 1)),
                         (vc_in[0], 16 * (J + 1)), (vc_in[1], 16 * (J + 1)), (bias_in[0], 16 * (J + 1)),
                         (bias_in[1], 16 * (J + 1)), (newk_stored, 16 * J + AHEAD),
                         (newv_stored, 16 * J), (att_stored[0], 32 * J + AHEAD), (att_stored[1], 32 * J + AHEAD)):
                sp.wait_ge(s, n)

        @block.gpsimd
        def _(pool):
            pool.dma_start(pd[:, 0:KD], v["normmT"]).then_inc(mean_stored, 16)
            nc.gpsimd.memset(pu[:], 0.0).then_inc(pool_step, 1)

            def make_lo(j, h):
                pool.wait_ge(k_hi_made, j * 2 + (h + 1))
                nc.gpsimd.tensor_tensor(kll[:, h, :], kraw[:], khh[:, h, :].bitcast(F32), ALU.subtract
                                        ).then_inc(k_lo_made, 1)

            def make_bias(j, h, first=False):
                pool.wait_ge(bias_in[h], j * 16 + 16)
                if not first:
                    pool.wait_ge(maxed, (j - 1) * maxed_before(U) + maxed_before(W * h + LW))
                b3 = brow[:, h, :].rearrange("p (a b) -> p a b", b=48)
                for rb in range(2):
                    for kind in range(3):
                        a0 = 4 * (1 - rb)
                        nc.gpsimd.tensor_tensor(
                            bias[:, h, 3 * rb + kind, :].rearrange("p (r c) -> p r c", c=KC),
                            b3[:, a0:a0 + KR, BOFF[kind]:BOFF[kind] + KC],
                            mask[:, 3 * rb + kind, :].rearrange("p (r c) -> p r c", c=KC), ALU.add
                        ).then_inc(bias_made, 1)

            make_lo(0, 0)
            pool.wait_ge(mask_in, 16)
            make_bias(0, 0, True)
            make_bias(0, 1, True)
            steps = 1
            for w in range(len(POOLW)):
                PER = w + 5
                pool.wait_ge(mean_stored, w * 32 + FIRST)
                pool.dma_start(inv[:], v["invcnt"][w:w + 1, :].broadcast_to([P, TOK])).then_inc(u_in, 16)
                base_u = w * (16 + 64) + 16
                with pool.Fori(0, 2) as i:
                    make_lo(i + 2 * w, 1)
                    pool.wait_ge(mean_stored, i * 16 + w * 32 + FIRST)
                    pool.wait_ge(pool_step, i * PER + steps)
                    for dst, src, n in SEG:
                        pool.dma_start(pu[:, dst:dst + n],
                                       projT[ds(i * P + (3 * NA_W + 2 * w * P), P), src:src + n]).then_inc(u_in, 16)
                    pool.wait_ge(u_in, i * 32 + (base_u + 32))
                    src = pu[:]
                    lo, hi = 0, PW
                    for m in range(w + 1):
                        a, b = (1, 0) if m == 0 else (1 << (m - 1), 1 << (m - 1))
                        lo, hi = lo + a, hi - b
                        dst = pc[:, m % 2, :]
                        if m:
                            pool.wait_ge(pool_step, i * PER + (steps + m))
                        nc.gpsimd.tensor_tensor(dst[:, lo:hi], src[:, lo - a:hi - a], src[:, lo + b:hi + b], ALU.add
                                                ).then_inc(pool_step, 1)
                        src = dst
                    pool.wait_ge(pool_step, i * PER + (steps + w + 1))
                    other = pc[:, (w + 1) % 2, :]
                    for s0, d0, ln in SEG:
                        nc.gpsimd.tensor_tensor(other[:, s0:s0 + ln], src[:, s0:s0 + ln], inv[:, d0:d0 + ln],
                                                ALU.mult).then_inc(pool_step, 1)
                    pool.wait_ge(pool_step, i * PER + (steps + w + 3))
                    for s0, d0, ln in SEG:
                        nc.gpsimd.tensor_tensor(pd[:, d0:d0 + ln], other[:, s0:s0 + ln], pu[:, s0:s0 + ln],
                                                ALU.subtract).then_inc(pool_step, 1)
                    pool.wait_ge(pool_step, i * PER + (steps + w + 5))
                    pool.dma_start(v["mean_d"][ds(i * P + 2 * w * P, P), :], pd[:]).then_inc(mean_stored, 16)
                    make_bias(i + (2 * w + 1), 0)
                    make_lo(i + (2 * w + 1), 0)
                    make_bias(i + (2 * w + 1), 1)
                steps += 2 * PER
            pool.wait_ge(mean_stored, 16 * 2 * len(POOLW) + FIRST)

        @block.scalar
        def _(act):
            def scale_q(j, h):
                act.wait_ge(kq_in, j * 192 + (96 * h + 96))
                act.wait_ge(q_lo_made, j * 2 + h)
                nc.scalar.activation(q8[:, 0:LAT].rearrange("p (b r c) -> p b r c", b=4, c=QC),
                                     qraw[:, 0:LAT].rearrange("p (r b c) -> p b r c", b=4, c=QC), ACT.Copy,
                                     scale=float(DH) ** -0.5).then_inc(q_scaled, 1)
                nc.scalar.activation(q8[:, LAT:TOK], qraw[:, LAT:TOK], ACT.Copy, scale=float(DH) ** -0.5
                                     ).then_inc(q_scaled, 1)

            def q_high(j, h, units):
                act.wait_ge(scored, units)
                act.wait_ge(q_scaled, j * 4 + (2 * h + 2))
                nc.scalar.activation(qst[:, h, :], q8[:], ACT.Copy).then_inc(q_hi_made, 1)

            def exps(j, u):
                s = u % 2
                act.wait_ge(negmax_ready, j * U + (u + 1))
                if u >= 3:
                    act.wait_ge(turned, j * U + (u - 3) + AHEAD)
                sums = st[:, u % 4, :]
                if unit(u)[1]:
                    nc.scalar.activation(pr[:, u % 4, 0:NKL], T[:, s, :], ACT.Exp, bias=sums[:, 2:3],
                                         accum_out=sums[:, 3:4])
                    nc.scalar.activation(pr[:, u % 4, NKL:NKEY], ps[:, 2 + s, :], ACT.Exp, bias=sums[:, 2:3],
                                         accum_out=sums[:, 4:5]).then_inc(exped, 1)
                else:
                    nc.scalar.activation(pr[:, u % 4, 0:CTX], ps[:, 2 + s, 0:CTX], ACT.Exp, bias=sums[:, 2:3],
                                         accum_out=sums[:, 5:6]).then_inc(exped, 1)

            def copy_a(j, u):
                act.wait_ge(turned, j * U + (u + 1) + AHEAD)
                if u:
                    act.wait_ge(valued, j * U + (u - 1) + AHEAD)
                n = 512 if unit(u)[1] else CTX
                nc.scalar.activation(prT[:, u % 2, 0:n], ps[:, 4, 0:n], ACT.Copy).then_inc(copied_a, 1)

            def read_batch(j, n, first=False):
                act.wait_ge(batch_turned, j * NB + (n + 1))
                if n < 4:
                    nc.scalar.activation(V[:, n, :, :], ps[:, 7, :].rearrange("p (r f) -> p r f", r=4), ACT.Copy
                                         ).then_inc(batch_read, 1)
                else:
                    if not first:
                        act.wait_ge(newk_stored, (j - 1) * 16 + AHEAD)
                        act.wait_ge(newv_stored, j * 16)
                    nc.scalar.activation(Kx[:], ps[:, 7, 0:CTX].rearrange("p (b f) -> p b f", b=CB), ACT.Copy)
                    nc.scalar.activation(Vx[:], ps[:, 7, CTX:2 * CTX].rearrange("p (b f) -> p b f", b=CB), ACT.Copy
                                         ).then_inc(batch_read, 1)

            scale_q(0, 0)
            q_high(0, 0, 0)
            for n in range(NB):
                read_batch(0, n, True)
            for u in range(3):
                exps(0, u)
            copy_a(0, 0)
            with act.Fori(0, J) as j:
                for u in range(U):
                    copy_a(j, u + 1)
                    exps(j, u + 3)
                    if u == 0:
                        scale_q(j, 1)
                    if u == 1:
                        q_high(j, 1, j * U + 1)
                    if u == 11:
                        scale_q(j + 1, 0)
                    if u == 12:
                        q_high(j + 1, 0, j * U + W)
                    if u in BATCH_AT:
                        read_batch(j + 1, BATCH_AT[u])
                read_batch(j + 1, 4)

        @block.vector
        def _(dve):
            def stats(j, u):
                s = u % 2
                h, latent, b = unit(u)
                m = maxed_before(u)
                maxima = st[:, u % 4, :]
                if u % W == 0:
                    dve.wait_ge(bias_made, j * 12 + 6 * (u // W + 1))
                dve.wait_ge(scored, j * U + (u + 1))
                n = 512 if latent else CTX
                nc.vector.tensor_reduce(maxima[:, 1:2], ps[:, 2 + s, 0:n], AX.X, ALU.max).then_inc(maxed, 1)
                if latent:
                    nc.vector.tensor_tensor_reduce(T[:, s, :], ps[:, s, 0:NKL],
                                                   bias[:, h, 3 * (b % 2) + KIND[b // 2], :], 1.0,
                                                   -3.0e38, ALU.add, ALU.max, maxima[:, 0:1]).then_inc(maxed, 1)
                    dve.wait_ge(maxed, j * maxed_before(U) + (m + 2))
                    nc.vector.tensor_scalar(maxima[:, 2:3], maxima[:, 0:1], maxima[:, 1:2], -1.0, ALU.max, ALU.mult
                                            ).then_inc(negmax_ready, 1)
                else:
                    dve.wait_ge(maxed, j * maxed_before(U) + (m + 1))
                    nc.vector.tensor_scalar(maxima[:, 2:3], maxima[:, 1:2], -1.0, None, ALU.mult
                                            ).then_inc(negmax_ready, 1)

            def normalise(j, u):
                s = u % 4
                latent = unit(u)[1]
                dve.wait_ge(exped, j * U + (u + 1))
                if latent:
                    nc.vector.tensor_tensor(st[:, s, 5:6], st[:, s, 3:4], st[:, s, 4:5], ALU.add
                                            ).then_inc(summed, 1)
                    dve.wait_ge(summed, j * (2 * LW) + (lat_before(u) + 1))
                if u >= 2:
                    dve.wait_ge(probs_ready, j * U + (u - 2) + AHEAD)
                nc.vector.reciprocal(st[:, s, 6:7], st[:, s, 5:6]).then_inc(inverted, 1)
                dve.wait_ge(inverted, j * U + (u + 1))
                n = NKEY if latent else CTX
                nc.vector.tensor_scalar(pr[:, s, 0:n], pr[:, s, 0:n], st[:, s, 6:7], None, ALU.mult
                                        ).then_inc(probs_ready, 1)

            def output(j, u):
                h, latent, b = unit(u)
                f = slice(h * DH, h * DH + DH)
                dve.wait_ge(valued, j * U + (u + 1) + AHEAD)
                if latent:
                    cb, rb = b // 2, b % 2
                    hi, lo = (a[f, 0:LAT].rearrange("p (r c) -> p r c", c=GRID_W)
                              [:, rb * QR:rb * QR + QR, cb * QC:cb * QC + QC] for a in (athi, atlo))
                    src = ps[f, 6, 0:P].rearrange("p (r c) -> p r c", c=QC)
                else:
                    hi, lo = (a[f, LAT + b * P:LAT + b * P + P] for a in (athi, atlo))
                    src = ps[f, 6, 0:P]
                if u % W == 0:
                    dve.wait_ge(att_stored[h], j * 32 + AHEAD)
                nc.vector.tensor_copy(hi, src).then_inc(out_hi, 1)
                dve.wait_ge(out_hi, j * U + (u + 1))
                nc.vector.tensor_tensor(lo, src, hi.bitcast(F32), ALU.subtract).then_inc(out_lo, 1)

            def lay_values(j):
                dve.wait_ge(v_in, j * 16 + 16)
                dve.wait_ge(batch_turned, j * NB)
                for cb in range(4):
                    nc.vector.tensor_copy(vL[:, cb * 512:cb * 512 + 512].rearrange("p (r c) -> p r c", c=KC),
                                          vT[:, 0:LAT].rearrange("p (r c) -> p r c", c=GRID_W)
                                          [:, :, COLB[cb]:COLB[cb] + KC]).then_inc(v_laid, 1)
                nc.vector.tensor_copy(vL[:, 4 * 512:], vT[:, LAT:TOK]).then_inc(v_laid, 1)

            def k_high(j, h, units):
                dve.wait_ge(kq_in, j * 192 + (96 * h + 96))
                dve.wait_ge(scored, units)
                nc.vector.tensor_copy(khh[:, h, :], kraw[:]).then_inc(k_hi_made, 1)

            def q_low(j, h):
                dve.wait_ge(q_hi_made, j * 2 + (h + 1))
                nc.vector.tensor_tensor(qst[DH:P, h, :], q8[DH:P, :], qst[DH:P, h, :].bitcast(F32), ALU.subtract
                                        ).then_inc(q_lo_made, 1)

            k_high(0, 0, 0)
            q_low(0, 0)
            lay_values(0)
            def copy_b(j, u):
                if unit(u)[1]:
                    dve.wait_ge(turned, j * U + (u + 1) + AHEAD)
                    if u:
                        dve.wait_ge(valued, j * U + (u - 1) + AHEAD)
                    nc.vector.tensor_copy(prT[:, u % 2, 512:NKEY], ps[:, 5, 0:NKEY - 512]).then_inc(copied_b, 1)

            stats(0, 0)
            stats(0, 1)
            normalise(0, 0)
            stats(0, 2)
            normalise(0, 1)
            copy_b(0, 0)
            with dve.Fori(0, J) as j:
                for u in range(U):
                    stats(j, u + 3)
                    copy_b(j, u + 1)
                    normalise(j, u + 2)
                    output(j, u)
                    if u == 2:
                        k_high(j, 1, j * U + 1)
                    if u in (4, 14):
                        q_low(j + u // 10, 1 - u // 10)
                    if u == 5:
                        lay_values(j + 1)
                    if u == 12:
                        k_high(j + 1, 0, j * U + W)

        @block.tensor
        def _(pe):
            def scores(j, u):
                s = u % 2
                h, latent, b = unit(u)
                if u >= 2:
                    pe.wait_ge(exped, j * U + (u - 1))
                if u % W == 0:
                    pe.wait_ge(q_lo_made, j * 2 + (u // W + 1))
                    pe.wait_ge(k_lo_made, j * 2 + (u // W + 1))
                if latent:
                    q = qst[:, h, b * P:b * P + P]
                    for n, k in enumerate((khh, kll)):
                        kw = k[:, h, 0:LAT].rearrange("p (r c) -> p r c", c=GRID_W)[
                            :, 4 * (b % 2):4 * (b % 2) + KR, COLB[b // 2]:COLB[b // 2] + KC]
                        nc.tensor.matmul(ps[:, s, 0:NKL], q, kw, start=(n == 0), stop=(n == 1))
                    for n, k in enumerate((khh, kll)):
                        last = nc.tensor.matmul(ps[:, 2 + s, :], q, k[:, h, TOK:KCOL], start=(n == 0), stop=(n == 1))
                else:
                    for n, k in enumerate((khh, kll)):
                        last = nc.tensor.matmul(ps[:, 2 + s, 0:CTX], qst[:, h, LAT + b * P:LAT + b * P + P],
                                                k[:, h, LAT:TOK], start=(n == 0), stop=(n == 1))
                last.then_inc(scored, 1)

            def turn(j, u):
                latent = unit(u)[1]
                if u:
                    pe.wait_ge(copied_a, j * U + u)
                    pe.wait_ge(copied_b, j * (2 * LW) + lat_before(u))
                pe.wait_ge(probs_ready, j * U + (u + 1) + AHEAD)
                for c in range(NKEY // P if latent else CB):
                    last = nc.tensor.transpose(ps[:, 4 + c // 4, (c % 4) * P:(c % 4) * P + P],
                                               pr[:, u % 4, c * P:c * P + P], ident[:])
                last.then_inc(turned, 1)

            def values(j, u):
                h, latent, b = unit(u)
                f = slice(h * DH, h * DH + DH)
                if u % W == 0:
                    pe.wait_ge(vc_in[h], j * 16 + 16)
                    pe.wait_ge(batch_read, j * NB + (NB - 1))
                if u == LW:
                    pe.wait_ge(batch_read, j * NB + NB)
                pe.wait_ge(copied_a, j * U + (u + 1))
                if latent:
                    pe.wait_ge(copied_b, j * (2 * LW) + (lat_before(u) + 1))
                    tiles = [V[:, b // 2, b % 2 + c, f] for c in range(3)]
                    tiles += [vc[:, c, f] for c in range(PAST // P)]
                else:
                    tiles = [Vx[:, c, f] for c in range(CB)]
                pe.wait_ge(out_lo, j * U + u + AHEAD)
                for c, t in enumerate(tiles):
                    last = nc.tensor.matmul(ps[f, 6, 0:P], t, prT[:, u % 2, c * P:c * P + P],
                                            start=(c == 0), stop=(c == len(tiles) - 1))
                last.then_inc(valued, 1)

            def batch(j, n, first=False):
                pe.wait_ge(batch_read, j * NB + n)
                if n == 0:
                    pe.wait_ge(v_laid, j * 5 + 5)
                if n < 4:
                    tiles = [vL[:, n * 512 + rg * P:n * 512 + rg * P + P] for rg in range(4)]
                else:
                    pe.wait_ge(kx_in, 16 if first else j * 16)
                    tiles = [kx[:, b * P:b * P + P] for b in range(CB)]
                    tiles += [vL[:, 4 * 512 + b * P:4 * 512 + b * P + P] for b in range(CB)]
                for c, t in enumerate(tiles):
                    last = nc.tensor.transpose(ps[:, 7, c * P:c * P + P], t, ident[:])
                last.then_inc(batch_turned, 1)

            for n in range(NB):
                batch(0, n, True)
            for u in range(3):
                scores(0, u)
            turn(0, 0)
            with pe.Fori(0, J) as j:
                for u in range(U):
                    scores(j, u + 3)
                    turn(j, u + 1)
                    values(j, u)
                    if u in BATCH_AT:
                        batch(j + 1, BATCH_AT[u])
                batch(j + 1, 4)


def output_projection(nc, sem, v):
    ps, ident, modT = v["ps"], v["ident"], v["modT"]
    xcat, w_out, y_d, mean_d, mixhi_d, mixlo_d = (v[n] for n in ("xcat", "w_out", "y_d", "mean_d", "mixhi_d", "mixlo_d"))
    NCH = D // CW
    NP = 4
    SLOTS = 2 * NP
    NG = len(POOLW)
    THIRDS = ((0, 512), (512, 512), (1024, 256))
    pool_consts = sem("o_pool_consts")
    mean_in = [sem(f"o_mean_in{s}") for s in range(2)]
    pooled = sem("o_pooled")
    pooled_scaled = sem("o_pooled_scaled")
    pooled_hi = sem("o_pooled_hi")
    pooled_lo = sem("o_pooled_lo")
    pooled_stored = [sem(f"o_pooled_stored{s}") for s in range(2)]
    gate_turned = sem("o_gate_turned")
    gate_read = sem("o_gate_read")
    mix_in = sem("o_mix_in")
    w_loaded = [sem(f"o_w_loaded{s}") for s in range(2)]
    w_hi_made = sem("o_w_hi_made")
    w_lo_made = sem("o_w_lo_made")
    piece_used = sem("o_piece_used")
    tile_done = sem("o_tile_done")
    gated = sem("o_gated")
    y_ready = sem("o_y_ready")
    x_in = [sem(f"o_x_in{s}") for s in range(2)]
    y_stored = [sem(f"o_y_stored{s}") for s in range(2)]
    with nc.sbuf_tensor("gate_row", [P, 2, D], F32) as gate_row:
        with ExitStack() as ctx:
            def sb(name, shape, dt=F32):
                return ctx.enter_context(nc.sbuf_tensor(name, shape, dt))
            wp = sb("wp", [P, 8, 256])
            psc = sb("psc", [P, 8])
            mean = sb("mean", [P, 2, 2, TOK])
            pl = sb("pl", [P, 2, TOK])
            plhi = sb("plhi", [P, 2, TOK], F32R)
            pllo = sb("pllo", [P, 2, TOK], F32R)
            block = ctx.enter_context(nc.Block())

            @block.sync
            def _(sp):
                sp.dma_start(wp[:], v["wpool"]).then_inc(pool_consts, 16)
                sp.dma_start(psc[:], v["poolsT"]).then_inc(pool_consts, 16)

                def load_mean(g):
                    sp.dma_start(mean[:, g % 2], mean_d[g * 256:g * 256 + 256, :].rearrange("(b p) t -> p b t", p=P)
                                 ).then_inc(mean_in[g % 2], 16)
                for g in range(2):
                    load_mean(g)
                for g in range(NG):
                    for b in range(2):
                        n = 2 * g + b
                        sp.wait_ge(pooled_lo, 3 * n + 3)
                        if b == 1 and g + 2 < NG:
                            load_mean(g + 2)
                        r = NA_W + n * P
                        sp.dma_start(mixhi_d[r:r + P, :], plhi[:, n % 2].bitcast(F32)).then_inc(pooled_stored[n % 2], 16)
                        sp.dma_start(mixlo_d[r:r + P, :], pllo[:, n % 2].bitcast(F32)).then_inc(pooled_stored[n % 2], 16)
                for s in range(2):
                    sp.wait_ge(pooled_stored[s], 4 * 32)

            @block.tensor
            def _(pe):
                for c in range(2):
                    for b in range(4):
                        if c:
                            pe.wait_ge(gate_read, b + 1)
                        for k in range(4):
                            col = modT[:, 32 + 4 * b + k, c:c + 1].broadcast_to([P, P])
                            last = nc.tensor.matmul(ps[:, b, k * P:k * P + P], col, ident[:], start=True, stop=True)
                        last.then_inc(gate_turned, 1)
                pe.wait_ge(pool_consts, 32)
                for g in range(NG):
                    pe.wait_ge(mean_in[g % 2], 16 * (g // 2 + 1))
                    for ob in range(2):
                        n = 2 * g + ob
                        for t, (t0, tn) in enumerate(THIRDS):
                            if n == 0 and t == 0:
                                pe.wait_ge(gate_read, 8)
                            if n >= 1:
                                pe.wait_ge(pooled_scaled, 3 * (n - 1) + t + 1)
                            for ib in range(2):
                                last = nc.tensor.matmul(ps[:, t, 0:tn], wp[:, 2 * g + ib, ob * P:ob * P + P],
                                                        mean[:, g % 2, ib, t0:t0 + tn], start=(ib == 0), stop=(ib == 1))
                            last.then_inc(pooled, 1)

            @block.scalar
            def _(act):
                for n in range(8):
                    for t, (t0, tn) in enumerate(THIRDS):
                        act.wait_ge(pooled_scaled, 3 * n + t + 1)
                        if n >= 2 and t == 0:
                            act.wait_ge(pooled_stored[n % 2], 32 * (n // 2))
                        nc.scalar.activation(plhi[:, n % 2, t0:t0 + tn], pl[:, n % 2, t0:t0 + tn], ACT.Copy
                                             ).then_inc(pooled_hi, 1)

            @block.vector
            def _(dve):
                for c in range(2):
                    for b in range(4):
                        dve.wait_ge(gate_turned, 4 * c + b + 1)
                        nc.vector.tensor_copy(gate_row[:, c, 512 * b:512 * b + 512], ps[:, b, :]).then_inc(gate_read, 1)
                dve.wait_ge(pool_consts, 32)
                for n in range(8):
                    for t, (t0, tn) in enumerate(THIRDS):
                        dve.wait_ge(pooled, 3 * n + t + 1)
                        if n >= 2:
                            dve.wait_ge(pooled_lo, 3 * (n - 2) + t + 1)
                        nc.vector.tensor_scalar(pl[:, n % 2, t0:t0 + tn], ps[:, t, 0:tn], psc[:, n:n + 1], None,
                                                ALU.mult).then_inc(pooled_scaled, 1)
                    for t, (t0, tn) in enumerate(THIRDS):
                        dve.wait_ge(pooled_hi, 3 * n + t + 1)
                        nc.vector.tensor_tensor(pllo[:, n % 2, t0:t0 + tn], pl[:, n % 2, t0:t0 + tn],
                                                plhi[:, n % 2, t0:t0 + tn].bitcast(F32), ALU.subtract
                                                ).then_inc(pooled_lo, 1)

        with ExitStack() as ctx:
            def sb(name, shape, dt=F32):
                return ctx.enter_context(nc.sbuf_tensor(name, shape, dt))
            mhi = sb("mhi", [P, KD, GT], F32R)
            mlo = sb("mlo", [P, KD, GT], F32R)
            raw = sb("o_raw", [P, 2, CH])
            whi = sb("o_whi", [P, 2, CH], F32R)
            wlo = sb("o_wlo", [P, 2, CH], F32R)
            xy = sb("o_xy", [P, 2, TPG, CW])
            tmp = sb("o_tmp", [P, 2, CW])
            block = ctx.enter_context(nc.Block())
            QP = CH // NP

            def slot(t, s):
                return t[:, s, :].rearrange("p (k n) -> p k n", k=KD)

            def tokens(dram, g, n):
                return dram[ds(g * GT, GT), ds(n * CW, CW)].rearrange("(t p) n -> p t n", p=P)

            @block.sync
            def _(sp):
                def load_w(g, n, s):
                    sp.wait_ge(w_lo_made, g * (NCH * NP) + n * NP + NP)
                    sp.dma_start(slot(raw, s), w_chunk(w_out, n * CW)).then_inc(w_loaded[s], 16)

                sp.sem_inc(y_ready, AHEAD)
                with sp.Fori(0, 2) as g:
                    sp.wait_ge(tile_done, g * (NCH * TPG) + 2 * TPG)
                    for q in range(4):
                        for dst, src in ((mhi, mixhi_d), (mlo, mixlo_d)):
                            sp.dma_start(dst[:, 4 * q:4 * q + 4, :].bitcast(F32),
                                         src[q * 512:q * 512 + 512, ds(g * GT, GT)].rearrange("(k p) t -> p k t", p=P)
                                         ).then_inc(mix_in, 16)
                        if q < 2:
                            load_w(g, q, q)
                    with sp.Fori(1, NCH // 2) as i:
                        for s in range(2):
                            load_w(g, i * 2 + s, s)

            @block.gpsimd
            def _(pool):
                def store_y(g, n, s):
                    pool.wait_ge(y_ready, g * (NCH * TPG) + n * TPG + TPG + AHEAD)
                    pool.dma_start(tokens(y_d, g, n), xy[:, s]).then_inc(y_stored[s], 16)

                for s in range(2):
                    pool.dma_start(xy[:, s, 0, 0:KD], v["normmT"]).then_inc(y_stored[s], 16)
                with pool.Fori(0, 2) as g:
                    for s in range(2):
                        pool.wait_ge(y_stored[s], g * (NCH * 8) + FIRST)
                        pool.dma_start(xy[:, s], tokens(xcat, g, s)).then_inc(x_in[s], 16)
                    with pool.Fori(0, NCH // 2 - 1) as i:
                        for s in range(2):
                            store_y(g, i * 2 + s, s)
                            pool.wait_ge(y_stored[s], g * (NCH * 8) + i * 16 + 16 + FIRST)
                            pool.dma_start(xy[:, s], tokens(xcat, g, i * 2 + (s + 2))).then_inc(x_in[s], 16)
                    for s in range(2):
                        store_y(g, NCH - 2 + s, s)
                for s in range(2):
                    pool.wait_ge(y_stored[s], NCH * 16 + FIRST)

            @block.scalar
            def _(act):
                with act.Fori(0, 2) as g:
                    with act.Fori(0, NCH // 2) as i:
                        for s in range(2):
                            act.wait_ge(w_loaded[s], g * (NCH * 8) + i * 16 + 16)
                            for q in range(NP):
                                if q < 3:
                                    act.wait_ge(piece_used, g * (NCH * 3) + i * 6 + (s * 3 + q + 1))
                                else:
                                    act.wait_ge(tile_done, g * (NCH * TPG) + i * (2 * TPG) + (s + 1) * TPG)
                                nc.scalar.activation(whi[:, s, q * QP:(q + 1) * QP], raw[:, s, q * QP:(q + 1) * QP],
                                                     ACT.Copy).then_inc(w_hi_made, 1)

            @block.vector
            def _(dve):
                for n, (what, credit) in enumerate(((piece_used, 6), (tile_done, 2 * TPG), (w_lo_made, SLOTS),
                                                    (gated, TPG))):
                    nc.vector.memset(tmp[:, 0, 64 * n:64 * n + 64], 0.0).then_inc(what, credit)
                dve.wait_ge(gated, TPG)

                def make_lo(g, n, s):
                    for q in range(NP):
                        dve.wait_ge(w_hi_made, g * (NCH * NP) + n * NP + (q + 1))
                        nc.vector.tensor_tensor(wlo[:, s, q * QP:(q + 1) * QP], raw[:, s, q * QP:(q + 1) * QP],
                                                whi[:, s, q * QP:(q + 1) * QP].bitcast(F32), ALU.subtract
                                                ).then_inc(w_lo_made, 1)

                def add_tile(g, n, t, s):
                    at = g * (NCH * TPG) + n * TPG + t
                    c = g if t >= 3 else 0
                    m = (s * TPG + t) % 2
                    if t == 0:
                        dve.wait_ge(x_in[s], g * (NCH * 8) + (n - s) * 8 + 16)
                    dve.wait_ge(tile_done, at + 1 + 2 * TPG)
                    if s or t >= 2:
                        dve.wait_ge(y_ready, at - 1 + AHEAD)
                    else:
                        dve.wait_ge(y_ready, g * (NCH * TPG) + n * TPG + AHEAD)
                    nc.vector.tensor_tensor(tmp[:, m, :], ps[:, t, 0:CW],
                                            gate_row[:, ds(c, 1), ds(n * CW, CW)].rearrange("p a n -> p (a n)"),
                                            ALU.mult).then_inc(gated, 1)
                    dve.wait_ge(gated, at + 1 + TPG)
                    nc.vector.tensor_tensor(xy[:, s, t, :], xy[:, s, t, :], tmp[:, m, :], ALU.add).then_inc(y_ready, 1)

                def chunk(g, n, s, following=True):
                    for t in range(TPG):
                        add_tile(g, n, t, s)
                        if t == 1 and following:
                            make_lo(g, n + 1, 1 - s)

                with dve.Fori(0, 2) as g:
                    make_lo(g, 0, 0)
                    with dve.Fori(0, NCH // 2 - 1) as i:
                        for s in range(2):
                            chunk(g, i * 2 + s, s)
                    chunk(g, NCH - 2, 0)
                    chunk(g, NCH - 1, 1, False)

            @block.tensor
            def _(pe):
                with pe.Fori(0, 2) as g:
                    with pe.Fori(0, NCH // 2) as i:
                        pe.wait_ge(mix_in, g * 128 + 128)
                        for s in range(2):
                            for t in range(TPG):
                                bank = ps[:, t, 0:CW]
                                pe.wait_ge(gated, g * (NCH * TPG) + i * (2 * TPG) + (s * TPG + t + 1))
                                for k in range(KD):
                                    if t == 0 and k % 4 == 0:
                                        pe.wait_ge(w_lo_made, g * (NCH * NP) + i * (2 * NP) + (s * NP + k // 4 + 1 + SLOTS))
                                    wh, wl = (w[:, s, k * CW:k * CW + CW] for w in (whi, wlo))
                                    mh, ml = (m[:, k, t * P:t * P + P] for m in (mhi, mlo))
                                    for j, (m, w) in enumerate(((mh, wh), (mh, wl), (ml, wh))):
                                        last = nc.tensor.matmul(bank, m, w, start=(k == 0 and j == 0),
                                                                stop=(k == KD - 1 and j == 2))
                                    if t == TPG - 1 and k % 4 == 3 and k < KD - 1:
                                        last.then_inc(piece_used, 1)
                                last.then_inc(tile_done, 1)


def router(nc, sem, v):
    ps, ident, modT, nfT, mulT, addT = (v[n] for n in ("ps", "ident", "modT", "nfT", "mulT", "addT"))
    y_d, xn_d = v["y_d"], v["xn_d"]
    NT = TOK // P
    consts_in = sem("r_consts_in")
    consts_made = sem("r_consts_made")
    y_in = [sem(f"r_y_in{s}") for s in range(2)]
    y_square = sem("r_y_square")
    y_rms = sem("r_y_rms")
    y_scaled = sem("r_y_scaled")
    y_turned = sem("r_y_turned")
    turned_read = sem("r_turned_read")
    logits_done = sem("r_logits_done")
    logits_read = sem("r_logits_read")
    xn_stored = [sem(f"r_xn_stored{s}") for s in range(2)]
    logits_turned = sem("r_logits_turned")
    soft_step = sem("r_soft_step")
    exps_made = sem("r_exps_made")
    aff_turned = sem("r_aff_turned")
    aff_read = sem("r_aff_read")
    pick_step = sem("r_pick_step")
    slots_turned = sem("r_slots_turned")
    PICKS_C = 3 * (CAP_C // 8) + 2
    PICKS = PICKS_C + 3 * (CAP_L // 8) + 2
    with ExitStack() as ctx:
        def sb(name, shape, dt=F32):
            return ctx.enter_context(nc.sbuf_tensor(name, shape, dt))
        yt = sb("r_yt", [P, 2, D])
        yT = sb("r_yT", [P, 2, D])
        junk = sb("r_junk", [P, 2, D])
        stat = sb("r_stat", [P, 2, 2])
        wr = sb("r_wr", [P, KD, E])
        wrm = sb("r_wrm", [P, 2, KD, E])
        shift_l = sb("r_shift_logits", [E, 2])
        logitsT = sb("r_logitsT", [E, TOK])
        soft = sb("r_soft", [P, NT, E])
        red = sb("r_red", [P, NT])
        inv = sb("r_inv", [P, NT])
        affL = sb("r_affL", [E, LAT])
        affC = sb("r_affC", [E, CTX])
        topL = sb("r_topL", [E, CAP_L])
        topC = sb("r_topC", [E, CAP_C])
        placeL = sb("r_placeL", [E, CAP_L], U32)
        placeC = sb("r_placeC", [E, CAP_C], U32)
        numL = sb("r_numL", [E, CAP_L])
        numC = sb("r_numC", [E, CAP_C])
        block = ctx.enter_context(nc.Block())
        cond = [1 if t * P >= LAT else 0 for t in range(NT)]

        @block.sync
        def _(sp):
            sp.dma_start(wr[:], v["wrT"]).then_inc(consts_in, 16)
            for t in range(NT):
                if t >= 2:
                    sp.wait_ge(xn_stored[t % 2], 16 * (t // 2))
                    sp.wait_ge(y_turned, 4 * (t - 1))
                sp.dma_start(yt[:, t % 2, :], y_d[t * P:t * P + P, :]).then_inc(y_in[t % 2], 16)

        @block.gpsimd
        def _(pool):
            for t in range(NT):
                pool.wait_ge(y_scaled, t + 1)
                pool.dma_start(xn_d[t * P:t * P + P, :], yt[:, t % 2, :]).then_inc(xn_stored[t % 2], 16)
            for s in range(2):
                pool.wait_ge(xn_stored[s], 16 * (NT // 2))

        @block.scalar
        def _(act):
            def square(t):
                act.wait_ge(y_in[t % 2], 16 * (t // 2 + 1))
                if t >= 2:
                    act.wait_ge(y_rms, 3 * (t - 1))
                nc.scalar.activation(junk[:, t % 2, :], yt[:, t % 2, :], ACT.Square, accum_out=stat[:, t % 2, 0:1]
                                     ).then_inc(y_square, 1)
                act.wait_ge(y_rms, 3 * t + 1)
                nc.scalar.activation(stat[:, t % 2, 1:2], stat[:, t % 2, 0:1], ACT.Sqrt).then_inc(y_rms, 1)

            square(0)
            for t in range(NT):
                if t + 1 < NT:
                    square(t + 1)
                for b in range(4):
                    act.wait_ge(y_turned, 4 * t + b + 1)
                    if t >= 2 and b == 0:
                        act.wait_ge(logits_done, t - 1)
                    nc.scalar.activation(yT[:, t % 2, 512 * b:512 * b + 512], ps[:, b, :], ACT.Copy
                                         ).then_inc(turned_read, 1)
            act.wait_ge(soft_step, 2)
            nc.scalar.activation(soft[:], soft[:], ACT.Exp).then_inc(exps_made, 1)

        @block.tensor
        def _(pe):
            pe.wait_ge(consts_made, 6)
            for k in range(KD):
                last = nc.tensor.matmul(ps[0:E, 6, 0:2], wr[:, k, :], addT[:, :, k], start=(k == 0),
                                        stop=(k == KD - 1))
            last.then_inc(logits_done, 1)

            def logits(t):
                pe.wait_ge(turned_read, 4 * t + 4)
                if t >= 2:
                    pe.wait_ge(logits_read, t)
                for k in range(KD):
                    last = nc.tensor.matmul(ps[0:E, 4 + t % 2, 0:P], wrm[:, cond[t], k, :],
                                            yT[:, t % 2, k * P:k * P + P], start=(k == 0), stop=(k == KD - 1))
                last.then_inc(logits_done, 1)

            for t in range(NT):
                pe.wait_ge(y_scaled, t + 1)
                for b in range(4):
                    if t:
                        pe.wait_ge(turned_read, 4 * (t - 1) + b + 1)
                    for k in range(4 * b, 4 * b + 4):
                        last = nc.tensor.transpose(ps[:, b, (k % 4) * P:(k % 4) * P + P],
                                                   yt[:, t % 2, k * P:k * P + P], ident[:])
                    last.then_inc(y_turned, 1)
                if t:
                    logits(t - 1)
            logits(NT - 1)
            pe.wait_ge(logits_read, NT + 1)
            for t in range(NT):
                last = nc.tensor.transpose(ps[:, 7, t * E:t * E + E], logitsT[:, t * P:t * P + P], ident[0:E, 0:E])
            last.then_inc(logits_turned, 1)
            pe.wait_ge(soft_step, 5)
            for b, tiles in enumerate(((0, 4), (4, 8), (8, 10))):
                for t in range(*tiles):
                    last = nc.tensor.transpose(ps[0:E, b, (t - tiles[0]) * P:(t - tiles[0] + 1) * P], soft[:, t, :],
                                               ident[:])
                last.then_inc(aff_turned, 1)
            for n, (src, size) in enumerate(((topC, CAP_C), (numC, CAP_C), (topL, CAP_L), (numL, CAP_L))):
                if n % 2 == 0:
                    pe.wait_ge(pick_step, PICKS_C if n == 0 else PICKS)
                nc.tensor.transpose(ps[0:size, 4 + n // 2, (n % 2) * E:(n % 2) * E + E], src[:], ident[0:E, 0:E]
                                    ).then_inc(slots_turned, 1)

        @block.vector
        def _(dve):
            for c in range(2):
                nc.vector.scalar_tensor_tensor(out=mulT[:, c, :], in0=modT[:, 4 * KD:5 * KD, c], scalar=1.0,
                                               in1=nfT[:], op0=ALU.add, op1=ALU.mult).then_inc(consts_made, 1)
                nc.vector.tensor_copy(addT[:, c, :], modT[:, 3 * KD:4 * KD, c]).then_inc(consts_made, 1)
            dve.wait_ge(consts_in, 16)
            dve.wait_ge(consts_made, 4)
            for c in range(2):
                nc.vector.tensor_tensor(wrm[:, c], wr[:], mulT[:, c, :].unsqueeze(2).broadcast_to([P, KD, E]),
                                        ALU.mult).then_inc(consts_made, 1)

            def scale_tile(t):
                st = stat[:, t % 2, :]
                dve.wait_ge(y_square, t + 1)
                nc.vector.tensor_scalar(st[:, 0:1], st[:, 0:1], 1.0 / D, EPS, ALU.mult, ALU.add).then_inc(y_rms, 1)
                dve.wait_ge(y_rms, 3 * t + 2)
                nc.vector.reciprocal(st[:, 0:1], st[:, 1:2]).then_inc(y_rms, 1)
                dve.wait_ge(y_rms, 3 * t + 3)
                nc.vector.tensor_scalar(yt[:, t % 2, :], yt[:, t % 2, :], st[:, 0:1], None, ALU.mult
                                        ).then_inc(y_scaled, 1)

            def add_shift(t):
                dve.wait_ge(logits_done, t + 2)
                nc.vector.tensor_scalar(logitsT[:, t * P:t * P + P], ps[0:E, 4 + t % 2, 0:P],
                                        shift_l[:, cond[t]:cond[t] + 1], None, ALU.add).then_inc(logits_read, 1)

            scale_tile(0)
            dve.wait_ge(logits_done, 1)
            nc.vector.tensor_copy(shift_l[:], ps[0:E, 6, 0:2]).then_inc(logits_read, 1)
            dve.wait_ge(logits_read, 1)
            for t in range(1, NT):
                scale_tile(t)
                add_shift(t - 1)
            add_shift(NT - 1)

            lt = ps[:, 7, 0:NT * E].rearrange("p (t e) -> p t e", e=E)
            dve.wait_ge(logits_turned, 1)
            nc.vector.tensor_reduce(red[:], lt, AX.X, ALU.max).then_inc(soft_step, 1)
            dve.wait_ge(soft_step, 1)
            nc.vector.tensor_tensor(soft[:], lt, red[:].unsqueeze(2).broadcast_to([P, NT, E]), ALU.subtract
                                    ).then_inc(soft_step, 1)
            dve.wait_ge(exps_made, 1)
            nc.vector.tensor_reduce(red[:], soft[:], AX.X, ALU.add).then_inc(soft_step, 1)
            dve.wait_ge(soft_step, 3)
            nc.vector.reciprocal(inv[:], red[:]).then_inc(soft_step, 1)
            dve.wait_ge(soft_step, 4)
            nc.vector.tensor_tensor(soft[:], soft[:], inv[:].unsqueeze(2).broadcast_to([P, NT, E]), ALU.mult
                                    ).then_inc(soft_step, 1)
            dve.wait_ge(aff_turned, 3)
            nc.vector.tensor_copy(affC[:], ps[0:E, 2, 0:CTX]).then_inc(aff_read, 1)
            for b in range(2):
                nc.vector.tensor_copy(affL[:, 512 * b:512 * b + 512], ps[0:E, b, :]).then_inc(aff_read, 1)
            dve.wait_ge(aff_read, 3)

            done = 0
            for aff, top, place, num, first, cap in ((affC, topC, placeC, numC, LAT, CAP_C),
                                                     (affL, topL, placeL, numL, 0, CAP_L)):
                for r in range(0, cap, 8):
                    if r:
                        dve.wait_ge(pick_step, done)
                    nc.vector.max(top[:, r:r + 8], aff[:]).then_inc(pick_step, 1)
                    dve.wait_ge(pick_step, done + 1)
                    nc.vector.max_index(place[:, r:r + 8], top[:, r:r + 8], aff[:]).then_inc(pick_step, 1)
                    dve.wait_ge(pick_step, done + 2)
                    nc.vector.match_replace(aff[:], top[:, r:r + 8], aff[:], -1.0).then_inc(pick_step, 1)
                    done += 3
                nc.vector.tensor_copy(num[:], place[:]).then_inc(pick_step, 1)
                dve.wait_ge(pick_step, done + 1)
                nc.vector.tensor_scalar(num[:], num[:], float(first), None, ALU.add).then_inc(pick_step, 1)
                done += 2
                dve.wait_ge(pick_step, done)
            for size, bank, gates, idx in ((CAP_C, 4, v["gC"], v["idxC"]), (CAP_L, 5, v["gL"], v["idxL"])):
                dve.wait_ge(slots_turned, 2 * (bank - 3))
                nc.vector.tensor_copy(gates[0:size, :], ps[0:size, bank, 0:E])
                nc.vector.tensor_copy(idx[0:size, 0:E], ps[0:size, bank, E:2 * E])
                nc.vector.tensor_copy(idx[0:size, E:E + 1], ps[0:size, bank, 2 * E - 1:2 * E])


def experts(nc, sem, v):
    ps, ident, modT, mulT, addT = (v[n] for n in ("ps", "ident", "modT", "mulT", "addT"))
    y_d, xn_d, idxL, idxC, gL, gC = (v[n] for n in ("y_d", "xn_d", "idxL", "idxC", "gL", "gC"))
    NUP = 2 * FE // CW
    DW = CH // KF
    ND = D // DW
    NCH = NUP + ND
    NP = 4
    EP = NCH * NP
    SLOTS = 2 * NP
    LO_COLS = 256
    NGR = 6
    GROUPS = [(3 * r, min(3 * r + 3, KD)) for r in range(NGR)]
    gate_turned = sem("e_gate_turned")
    gate_read = sem("e_gate_read")
    index_set = sem("e_index_set")
    gathered = sem("e_gathered")
    xs_turned = sem("e_xs_turned")
    xs_step = sem("e_xs_step")
    xs_hi = sem("e_xs_hi")
    xs_made = sem("e_xs_made")
    w_loaded = [sem(f"e_w_loaded{s}") for s in range(2)]
    w_hi_made = sem("e_w_hi_made")
    w_lo_made = sem("e_w_lo_made")
    piece_used = sem("e_piece_used")
    sum_read = sem("e_sum_read")
    sum_copied = sem("e_sum_copied")
    silu_made = sem("e_silu_made")
    h_made = sem("e_h_made")
    h_hi = sem("e_h_hi")
    h_lo = sem("e_h_lo")
    ys_made = sem("e_ys_made")
    affinity_set = sem("e_affinity_set")
    scattered = sem("e_scattered")
    with ExitStack() as ctx:
        def sb(name, shape, dt=F32):
            return ctx.enter_context(nc.sbuf_tensor(name, shape, dt))
        gate_row = sb("e_gate_row", [P, 2, D])
        raw = sb("e_raw", [P, 2, CH])
        whi = sb("e_whi", [P, 2, CH], F32R)
        wlo = sb("e_wlo", [P, 2, CH], F32R)
        xg_l = sb("e_xg_l", [P, D])
        xg_c = sb("e_xg_c", [CAP_C, D])
        xs = sb("e_xs", [P, KD, 2 * CAP], F32R)
        tmp = sb("e_tmp", [P, 2, 3, CAP])
        gsum = sb("e_gsum", [P, 2, CAP])
        usum = sb("e_usum", [P, 2, CAP])
        gact = sb("e_gact", [P, 2, CAP])
        hf = sb("e_hf", [P, 2, CAP])
        h = sb("e_h", [P, KF, 2 * CAP], F32R)
        ys_l = sb("e_ys_l", [P, D])
        ys_c = sb("e_ys_c", [CAP_C, D])
        index_l = sb("e_index_l", [P, 1], U32)
        index_c = sb("e_index_c", [CAP_C, 1], U32)
        carried = sb("e_carried", [P, 1])
        aff_l = sb("e_aff_l", [P, 1])
        aff_c = sb("e_aff_c", [CAP_C, 1])
        block = ctx.enter_context(nc.Block())

        def piece(t, c, q):
            if c % NCH < NUP:
                b, half = divmod(q, 2)
                return t[:, c % 2, :].rearrange("p (k n) -> p k n", k=KD)[:, half * 8:half * 8 + 8, b * P:b * P + P]
            return t[:, c % 2, q * 1024:q * 1024 + 1024].rearrange("p (k n) -> p k n", k=8)

        @block.sync
        def _(sp):
            for s in (h_made, sum_read, ys_made):
                sp.sem_inc(s, AHEAD)
            with sp.Fori(0, E) as e:
                for c in range(NCH):
                    if c < NUP:
                        w, col, kb, width = v["w_up" if c % 2 else "w_gate"], (c // 2) * CW, KD, CW
                    else:
                        w, col, kb, width = v["w_down"], (c - NUP) * DW, KF, DW
                    sp.wait_ge(w_lo_made, e * EP + c * NP + NP)
                    sp.dma_start(raw[:, c % 2, :].rearrange("p (k n) -> p k n", k=kb),
                                 w[ds(e, 1), :, col:col + width].rearrange("a (k p) n -> p (a k) n", p=P)
                                 ).then_inc(w_loaded[c % 2], 16)

        @block.gpsimd
        def _(pool):
            def set_index(e):
                nc.gpsimd.tensor_copy(index_l[:], idxL[:, ds(e, 1)]).then_inc(index_set, 1)
                nc.gpsimd.tensor_copy(index_c[:], idxC[0:CAP_C, ds(e, 1)]).then_inc(index_set, 1)

            def carry_waits():
                nc.gpsimd.tensor_tensor(carried[:], ident[:, 0:1], ident[:, 0:1], ALU.add)

            def gather():
                nc.gpsimd.indirect_dma_start(xg_l[:], None, xn_d, bass.IndirectOffsetOnAxis(index_l[:, 0:1], 0)
                                             ).then_inc(gathered, 16)
                nc.gpsimd.indirect_dma_start(xg_c[:], None, xn_d, bass.IndirectOffsetOnAxis(index_c[:, 0:1], 0)
                                             ).then_inc(gathered, 16)

            def add_to_y(e, indices_set):
                set_index(e)
                pool.wait_ge(index_set, indices_set)
                pool.wait_ge(ys_made, e * (2 * ND) + 2 * ND + AHEAD)
                carry_waits()
                for rows, index in ((ys_l, index_l), (ys_c, index_c)):
                    nc.gpsimd.indirect_dma_start(y_d, bass.IndirectOffsetOnAxis(index[:, 0:1], 0), rows[:], None,
                                                 compute_op=ALU.add).then_inc(scattered, 16)

            pool.dma_start(ys_l[:, 0:KD], v["normfT"]).then_inc(scattered, 16)
            set_index(0)
            pool.wait_ge(index_set, 2)
            gather()
            with pool.Fori(0, E - 1) as e:
                pool.wait_ge(xs_turned, e * NGR + NGR)
                pool.wait_ge(scattered, e * 32 + FIRST)
                set_index(e + 1)
                pool.wait_ge(index_set, e * 4 + 4)
                carry_waits()
                gather()
                pool.wait_ge(gathered, e * 32 + 64)
                add_to_y(e, e * 4 + 6)
            pool.wait_ge(scattered, 32 * (E - 1) + FIRST)
            add_to_y(E - 1, 4 * E)
            pool.wait_ge(scattered, 32 * E + FIRST)

        @block.scalar
        def _(act):
            def make_hi(e, c, pieces):
                for q in pieces:
                    if q == 0:
                        act.wait_ge(w_loaded[c % 2], e * (NCH * 8) + (c // 2) * 16 + 16)
                    recut = c % NCH in (0, 1, NUP, NUP + 1)
                    act.wait_ge(piece_used, e * EP + c * NP + (NP if recut else q + 1))
                    nc.scalar.activation(piece(whi, c, q), piece(raw, c, q), ACT.Copy).then_inc(w_hi_made, 1)

            def xs_high(n, groups):
                for r in groups:
                    k0, k1 = GROUPS[r]
                    act.wait_ge(xs_step, n * (4 * NGR) + 4 * r + 4)
                    nc.scalar.activation(xs[:, k0:k1, 0:CAP], tmp[:, r % 2, 0:k1 - k0, :], ACT.Copy
                                         ).then_inc(xs_hi, 1)

            def silu(e, j, b):
                act.wait_ge(sum_read, e * (2 * NUP) + 4 * j + b + 1 + AHEAD)
                nc.scalar.activation(gact[:, b, :], gsum[:, b, :], ACT.Silu).then_inc(silu_made, 1)

            def h_high(e, j, b):
                act.wait_ge(h_made, e * KF + 2 * j + b + 1 + AHEAD)
                nc.scalar.activation(h[:, 2 * j + b, 0:CAP], hf[:, b, :], ACT.Copy).then_inc(h_hi, 1)

            def expert(e, last=False):
                for c in range(NCH):
                    following = c < NCH - 1 or not last
                    if following:
                        make_hi(e, c + 1, (0, 1))
                    if c < NUP:
                        j = c // 2
                        if c % 2 == 0:
                            if j:
                                h_high(e, j - 1, 1)
                            silu(e, j, 0)
                        else:
                            silu(e, j, 1)
                            h_high(e, j, 0)
                    elif c == NUP:
                        h_high(e, KF // 2 - 1, 1)
                    if following:
                        make_hi(e, c + 1, (2, 3))
                    if c in (NUP + 1, NUP + 2) and not last:
                        xs_high(e + 1, range(3) if c == NUP + 1 else range(3, NGR))

            make_hi(0, 0, range(NP))
            xs_high(0, range(NGR))
            with act.Fori(0, E - 1) as e:
                expert(e)
            expert(E - 1, True)

        @block.vector
        def _(dve):
            nc.vector.memset(tmp[:, 0, 0, :], 0.0).then_inc(piece_used, SLOTS)
            nc.vector.memset(tmp[:, 0, 1, :], 0.0).then_inc(w_lo_made, SLOTS)
            for c in range(2):
                for b in range(4):
                    dve.wait_ge(gate_turned, 4 * c + b + 1)
                    nc.vector.tensor_copy(gate_row[:, c, 512 * b:512 * b + 512], ps[:, 4 + b, :]).then_inc(gate_read, 1)

            def make_lo(e, c, pieces):
                for q in pieces:
                    dve.wait_ge(w_hi_made, e * EP + c * NP + (q + 1))
                    nc.vector.tensor_tensor(piece(wlo, c, q), piece(raw, c, q), piece(whi, c, q).bitcast(F32),
                                            ALU.subtract).then_inc(w_lo_made, 1)

            def build_xs(n, groups):
                for r in groups:
                    k0, k1 = GROUPS[r]
                    nk = k1 - k0
                    turned = ps[:, r % 3, 0:nk * CAP].rearrange("p (k n) -> p k n", k=nk)
                    t3 = tmp[:, r % 2, 0:nk, :]
                    dve.wait_ge(xs_turned, n * NGR + r + 1)
                    if r >= 2:
                        dve.wait_ge(xs_made, n * NGR + r - 1)
                    else:
                        dve.wait_ge(xs_made, n * NGR)
                    parts = ((0, slice(0, CAP_L), CAP_L), (1, slice(CAP_L, CAP), CAP_C))
                    for c, at, size in parts:
                        nc.vector.tensor_tensor(t3[:, :, at], turned[:, :, at],
                                                mulT[:, c, k0:k1].unsqueeze(2).broadcast_to([P, nk, size]), ALU.mult
                                                ).then_inc(xs_step, 1)
                    for c, at, size in parts:
                        dve.wait_ge(xs_step, n * (4 * NGR) + 4 * r + c + 1)
                        nc.vector.tensor_tensor(t3[:, :, at], t3[:, :, at],
                                                addT[:, c, k0:k1].unsqueeze(2).broadcast_to([P, nk, size]), ALU.add
                                                ).then_inc(xs_step, 1)
                    dve.wait_ge(xs_hi, n * NGR + r + 1)
                    nc.vector.tensor_tensor(xs[:, k0:k1, CAP:2 * CAP], t3, xs[:, k0:k1, 0:CAP].bitcast(F32),
                                            ALU.subtract).then_inc(xs_made, 1)

            def add_halves(e, j, what, b):
                bank = 2 * what + b
                dve.wait_ge(piece_used, e * EP + (2 * j + what) * NP + 2 * b + 2 + SLOTS)
                if what and j:
                    dve.wait_ge(h_made, e * KF + 2 * (j - 1) + b + 1 + AHEAD)
                elif what:
                    dve.wait_ge(h_made, e * KF + AHEAD)
                out = (gsum, usum)[what][:, b, :]
                nc.vector.tensor_copy(out, ps[:, bank, CAP:2 * CAP]).then_inc(sum_copied, 1)
                dve.wait_ge(sum_copied, e * (2 * NUP) + 4 * j + bank + 1)
                nc.vector.tensor_tensor(out, out, ps[:, bank, 0:CAP], ALU.add).then_inc(sum_read, 1)

            def multiply(e, j, b):
                dve.wait_ge(silu_made, e * KF + 2 * j + b + 1)
                dve.wait_ge(sum_read, e * (2 * NUP) + 4 * j + 2 + b + 1 + AHEAD)
                nc.vector.tensor_tensor(hf[:, b, :], gact[:, b, :], usum[:, b, :], ALU.mult).then_inc(h_made, 1)

            def h_low(e, j, b):
                dve.wait_ge(h_hi, e * KF + 2 * j + b + 1)
                nc.vector.tensor_tensor(h[:, 2 * j + b, CAP:2 * CAP], hf[:, b, :],
                                        h[:, 2 * j + b, 0:CAP].bitcast(F32), ALU.subtract).then_inc(h_lo, 1)

            def scale_ys(e, d):
                dve.wait_ge(piece_used, e * EP + (NUP + d) * NP + NP + SLOTS)
                for c, (ys, aff, size) in enumerate(((ys_l, aff_l, CAP_L), (ys_c, aff_c, CAP_C))):
                    cols = slice(d * DW, d * DW + DW)
                    nc.vector.scalar_tensor_tensor(out=ys[:, cols], in0=ps[0:size, 4 + (d % 2) * 2 + c, :],
                                                   scalar=aff[:, 0:1], in1=gate_row[0:size, c, cols], op0=ALU.mult,
                                                   op1=ALU.mult).then_inc(ys_made, 1)

            def expert(e, last=False):
                for c in range(NCH):
                    following = c < NCH - 1 or not last
                    if following:
                        make_lo(e, c + 1, (0, 1))
                    if c < NUP:
                        j = c // 2
                        if c % 2 == 0:
                            if j:
                                h_low(e, j - 1, 1)
                            add_halves(e, j, 0, 0)
                        else:
                            add_halves(e, j, 1, 0)
                            multiply(e, j, 0)
                    elif c == NUP:
                        h_low(e, KF // 2 - 1, 1)
                        dve.wait_ge(scattered, e * 32 + FIRST)
                        nc.vector.tensor_copy(aff_l[:], gL[:, ds(e, 1)]).then_inc(affinity_set, 1)
                        nc.vector.tensor_copy(aff_c[:], gC[0:CAP_C, ds(e, 1)]).then_inc(affinity_set, 1)
                        dve.wait_ge(affinity_set, e * 2 + 2)
                    else:
                        scale_ys(e, c - NUP - 1)
                    if following:
                        make_lo(e, c + 1, (2, 3))
                    if c < NUP:
                        if c % 2 == 0:
                            add_halves(e, j, 0, 1)
                        else:
                            h_low(e, j, 0)
                            add_halves(e, j, 1, 1)
                            multiply(e, j, 1)
                    elif c in (NUP + 1, NUP + 2) and not last:
                        build_xs(e + 1, range(3) if c == NUP + 1 else range(3, NGR))
                scale_ys(e, ND - 1)

            make_lo(0, 0, range(NP))
            build_xs(0, range(NGR))
            with dve.Fori(0, E - 1) as e:
                expert(e)
            expert(E - 1, True)

        @block.tensor
        def _(pe):
            for c in range(2):
                for b in range(4):
                    if c:
                        pe.wait_ge(gate_read, b + 1)
                    for k in range(4):
                        col = modT[:, 5 * KD + 4 * b + k, c:c + 1].broadcast_to([P, P])
                        last = nc.tensor.matmul(ps[:, 4 + b, k * P:k * P + P], col, ident[:], start=True, stop=True)
                    last.then_inc(gate_turned, 1)

            def turn_xs(n, groups, banks_free):
                pe.wait_ge(gathered, n * 32 + 32)
                for r in groups:
                    k0, k1 = GROUPS[r]
                    if r >= 3:
                        pe.wait_ge(xs_step, n * (4 * NGR) + 4 * (r - 3) + 4)
                    elif banks_free is not None and r == 0:
                        pe.wait_ge(sum_read, banks_free + AHEAD)
                    for k in range(k0, k1):
                        at = (k - k0) * CAP
                        nc.tensor.transpose(ps[:, r % 3, at:at + CAP_L], xg_l[:, k * P:k * P + P], ident[:])
                        last = nc.tensor.transpose(ps[:, r % 3, at + CAP_L:at + CAP], xg_c[:, k * P:k * P + P],
                                                   ident[0:CAP_C, 0:CAP_C])
                    last.then_inc(xs_turned, 1)

            def expert(e, last_expert=False):
                for c in range(NCH):
                    s = c % 2
                    done = e * EP + c * NP + SLOTS
                    if c < NUP:
                        j = c // 2
                        if c == 0:
                            pe.wait_ge(xs_made, e * NGR + NGR)
                            pe.wait_ge(sum_read, e * (2 * NUP) + AHEAD)
                        for b in range(2):
                            bank = ps[:, 2 * s + b, :]
                            if j:
                                pe.wait_ge(sum_read, e * (2 * NUP) + 4 * (j - 1) + 2 * s + b + 1 + AHEAD)
                            for k in range(KD):
                                if k % 8 == 0:
                                    pe.wait_ge(w_lo_made, done + 2 * b + k // 8 + 1)
                                at = k * CW + b * P
                                parts = [(whi, 2 * CAP), (wlo, LO_COLS)]
                                for w, cols in parts if k < KD - 1 else parts[::-1]:
                                    last = nc.tensor.matmul(bank[:, 0:cols], w[:, s, at:at + P], xs[:, k, 0:cols],
                                                            start=(k == 0 and w is whi),
                                                            stop=(k == KD - 1 and w is whi))
                                if k % 8 == 7:
                                    last.then_inc(piece_used, 1)
                    else:
                        d = c - NUP
                        bl, bc = (ps[:, 4 + (d % 2) * 2, :], ps[0:CAP_C, 5 + (d % 2) * 2, :])
                        pe.wait_ge(ys_made, e * (2 * ND) + (2 * (d - 1) if d >= 2 else 0) + AHEAD)
                        for k in range(KF):
                            if d == 0:
                                pe.wait_ge(h_lo, e * KF + k + 1)
                            if k % 2 == 0:
                                pe.wait_ge(w_lo_made, done + k // 2 + 1)
                            wh, wl = (w[:, s, k * DW:k * DW + DW] for w in (whi, wlo))
                            for bank, a0, size in ((bl, 0, CAP_L), (bc, CAP_L, CAP_C)):
                                hh, hl = (h[:, k, a:a + size] for a in (a0, CAP + a0))
                                for i, (x, w) in enumerate(((hh, wh), (hh, wl), (hl, wh))):
                                    last = nc.tensor.matmul(bank, x, w, start=(k == 0 and i == 0),
                                                            stop=(k == KF - 1 and i == 2))
                            if k % 2 == 1:
                                last.then_inc(piece_used, 1)
                        if d < 2 and not last_expert:
                            turn_xs(e + 1, range(3) if d == 0 else range(3, NGR), (e + 1) * (2 * NUP))

            turn_xs(0, range(NGR), None)
            pe.wait_ge(gate_read, 8)
            with pe.Fori(0, E - 1) as e:
                expert(e)
            expert(E - 1, True)


def final_norm(nc, sem, v):
    y_d, nfin = v["y_d"], v["nfin"]
    NT = TOK // P
    SL = 3
    gain_in = sem("f_gain_in")
    y_in = [sem(f"f_y_in{s}") for s in range(SL)]
    y_square = sem("f_y_square")
    y_rms = sem("f_y_rms")
    y_made = sem("f_y_made")
    stored = [sem(f"f_stored{s}") for s in range(SL)]
    with ExitStack() as ctx:
        def sb(name, shape, dt=F32):
            return ctx.enter_context(nc.sbuf_tensor(name, shape, dt))
        gain = sb("f_gain", [P, D])
        yt = sb("f_yt", [P, SL, D])
        out = sb("f_out", [P, SL, D])
        junk = sb("f_junk", [P, 2, D])
        stat = sb("f_stat", [P, 2, 2])
        block = ctx.enter_context(nc.Block())

        @block.sync
        def _(sp):
            for t in range(NT):
                if t >= SL:
                    sp.wait_ge(y_made, t - SL + 1)
                sp.dma_start(yt[:, t % SL, :], y_d[t * P:t * P + P, :]).then_inc(y_in[t % SL], 16)
                if t == 0:
                    sp.dma_start(gain[:], nfin.broadcast_to([P, D])).then_inc(gain_in, 16)

        @block.gpsimd
        def _(pool):
            for t in range(NT):
                pool.wait_ge(y_made, t + 1)
                rows = v["y_sample"][t * P:t * P + P, :] if t * P < LAT else v["y_prompt"][t * P - LAT:t * P - LAT + P, :]
                pool.dma_start(rows, out[:, t % SL, :]).then_inc(stored[t % SL], 16)
            for s in range(SL):
                pool.wait_ge(stored[s], 16 * len(range(s, NT, SL)))

        @block.scalar
        def _(act):
            for t in range(NT):
                act.wait_ge(y_in[t % SL], 16 * (t // SL + 1))
                if t >= 2:
                    act.wait_ge(y_rms, 3 * (t - 1))
                nc.scalar.activation(junk[:, t % 2, :], yt[:, t % SL, :], ACT.Square, accum_out=stat[:, t % 2, 0:1]
                                     ).then_inc(y_square, 1)
                act.wait_ge(y_rms, 3 * t + 1)
                nc.scalar.activation(stat[:, t % 2, 1:2], stat[:, t % 2, 0:1], ACT.Sqrt).then_inc(y_rms, 1)

        @block.vector
        def _(dve):
            dve.wait_ge(gain_in, 16)
            for t in range(NT):
                st = stat[:, t % 2, :]
                dve.wait_ge(y_square, t + 1)
                nc.vector.tensor_scalar(st[:, 0:1], st[:, 0:1], 1.0 / D, EPS, ALU.mult, ALU.add).then_inc(y_rms, 1)
                dve.wait_ge(y_rms, 3 * t + 2)
                nc.vector.reciprocal(st[:, 0:1], st[:, 1:2]).then_inc(y_rms, 1)
                dve.wait_ge(y_rms, 3 * t + 3)
                if t >= SL:
                    dve.wait_ge(stored[t % SL], 16 * (t // SL))
                nc.vector.scalar_tensor_tensor(out=out[:, t % SL, :], in0=yt[:, t % SL, :], scalar=st[:, 0:1],
                                               in1=gain[:], op0=ALU.mult, op1=ALU.mult).then_inc(y_made, 1)


INS = ['xcat', 'condT', 'bmodT', 'normmT', 'normfT', 'nfin', 'poolsT', 'w_mod', 'w_in', 'wpool', 'w_out',
       'wrT', 'w_gate', 'w_up', 'w_down', 'kcT', 'vcache', 'biasE', 'masks', 'invcnt', 'identity']
OUTS = ['y_prompt', 'y_sample', 'new_k', 'new_v']
OUT_SHAPES = [(CTX, D), (LAT, D), (CTX, NA_W), (CTX, NA_W)]


def window_masks():
    m = np.full((P, 2, 3, NKL), -1e30, np.float32)
    for rb in range(2):
        for kind, qc0, kc0 in ((0, 0, 0), (1, 16, 8), (2, 48, 32)):
            for r in range(QR):
                for c in range(QC):
                    qr, qc = rb * QR + r, qc0 + c
                    r0 = min(max(qr - WIN_R // 2, 0), ROWS - WIN_R)
                    c0 = min(max(qc - WIN_C // 2, 0), GRID_W - WIN_C)
                    row = m[r * QC + c, rb, kind].reshape(KR, KC)
                    row[r0 - 4 * rb:r0 - 4 * rb + WIN_R, c0 - kc0:c0 - kc0 + WIN_C] = 0.0
    return m.reshape(P, 6, NKL)


def inverse_counts():
    rows = []
    for w in POOLW:
        row = []
        for n in (LAT, CTX):
            t = np.arange(n)
            row.append(1.0 / (np.minimum(t + w - w // 2, n) - np.maximum(t - w // 2, 0)))
        rows.append(np.concatenate(row))
    return np.stack(rows).astype(np.float32)


def bias_rows(rpb):
    pad = np.pad(rpb, ((0, 0), (4, 4), (16, 17)))
    out = np.empty((H, QR, QC, 16, 48), rpb.dtype)
    for r in range(QR):
        for c in range(QC):
            out[:, r, c] = pad[:, 7 - r:23 - r, 15 - c:63 - c]
    return out.reshape(H, P, 16 * 48)


def columns(a, n):
    return np.ascontiguousarray(np.asarray(a).reshape(n, P).T)


def host_layout(x_prompt, x_sample, cache_k, cache_v, c, c_ctx, w_mod, b_mod, norm_mix, norm_ffn, w_in, rpb,
                w_pool, pool_scale, w_out, w_router, w_gate, w_up, w_down, norm_final):
    a = {}
    a['xcat'] = np.concatenate([x_sample[0], x_prompt[0]], 0)
    a['condT'] = np.stack([columns(c[0], KD), columns(c_ctx, KD)], 2)
    b = columns(b_mod[0], 96)
    a['bmodT'] = np.stack([b, b], 2)
    a['normmT'] = columns(norm_mix[0], KD)
    a['normfT'] = columns(norm_ffn[0], KD)
    a['nfin'] = norm_final.reshape(1, D)
    a['poolsT'] = columns(pool_scale[0], 8)
    a['w_mod'] = w_mod[0]
    a['w_in'] = w_in[0]
    a['wpool'] = w_pool[0].reshape(8, P, 256).transpose(1, 0, 2)
    a['w_out'] = w_out[0]
    a['wrT'] = w_router[0].reshape(KD, P, E).transpose(1, 0, 2)
    a['w_gate'], a['w_up'], a['w_down'] = w_gate[0], w_up[0], w_down[0]
    a['kcT'] = np.pad(cache_k[0, 0].reshape(PAST, NA_W).T, ((0, P), (0, 0)))
    a['vcache'] = np.pad(cache_v[0, 0].reshape(PAST, NA_W), ((0, 0), (0, P)))
    a['biasE'] = np.pad(bias_rows(rpb[0]), ((0, 2), (0, 0), (0, 0)))
    a['masks'] = window_masks()
    a['invcnt'] = inverse_counts()
    a['identity'] = np.eye(P, dtype=np.float32)
    return {n: np.ascontiguousarray(a[n]) for n in INS}


def kernel(**inputs):
    import concourse.bacc as _bacc
    from concourse.bass_utils import run_bass_kernel_spmd as _run

    arrays = host_layout(**{n: np.asarray(x) for n, x in inputs.items()})
    nc = _bacc.Bacc("TRN2", target_bir_lowering=False, num_devices=1)
    ins = [nc.dram_tensor(f"in_{n}", arrays[n].shape, mybir.dt.from_np(arrays[n].dtype),
                          kind="ExternalInput").ap() for n in INS]
    outs = [nc.dram_tensor(f"out_{n}", s, F32, kind="ExternalOutput").ap() for n, s in zip(OUTS, OUT_SHAPES)]
    block_diffusion_step(nc, *ins, *outs)
    r = _run(nc, [{f"in_{n}": arrays[n] for n in INS}], core_ids=[0])
    got = {n: r.results[0][f"out_{n}"] for n in OUTS}
    return (got['y_prompt'].reshape(1, CTX, D), got['y_sample'].reshape(1, LAT, D),
            got['new_k'].reshape(1, 1, CTX, H, DH), got['new_v'].reshape(1, 1, CTX, H, DH))
```
